# Optimizing a Trainium2 kernel written in Bass

```python
import math
import jax, jax.numpy as jnp
from jax import lax
import numpy as np

D_MODEL = 1024
BATCH = 1
SEQ = 256
DEPTH = 2
DEC_BATCH = 1
DEC_SEQ = 512
PAST_LEN = 128

GRID_W = 64
HEAD_DIM = 64
AXIAL_DIM = HEAD_DIM // 2
GQA_HEADS = 8
GQA_KV_HEADS = 2
GQA_GROUP = GQA_HEADS // GQA_KV_HEADS
DIFF_HEADS = 4
DIFF_V_DIM = 2 * HEAD_DIM
GQA_Q = GQA_HEADS * HEAD_DIM
GQA_KV = GQA_KV_HEADS * HEAD_DIM
DIFF_QK = DIFF_HEADS * 2 * HEAD_DIM
DIFF_V = DIFF_HEADS * DIFF_V_DIM
MIX_WIDTH = GQA_Q + DIFF_V
IN_WIDTH = GQA_Q + 2 * GQA_KV + 2 * DIFF_QK + DIFF_V
SPLITS = (GQA_Q, GQA_Q + GQA_KV, GQA_Q + 2 * GQA_KV, GQA_Q + 2 * GQA_KV + DIFF_QK, GQA_Q + 2 * GQA_KV + 2 * DIFF_QK)
D_FF = ((8 * D_MODEL + 3 * 256 - 1) // (3 * 256)) * 256
ROPE_THETA = 10000.0
Q_BLOCK = 128
NORM_EPS = 1e-6
DIFF_NORM_EPS = 1e-5

kernel_name = "hybrid_gqa_axial_diffattn_encoder"

def rms_norm(x, g, eps):
    xf = x.astype(jnp.float32)
    y = xf * lax.rsqrt(jnp.mean(xf * xf, axis=-1, keepdims=True) + eps)
    return (y * g.astype(jnp.float32)).astype(x.dtype)

def rope_angles(pos, dim):
    inv = ROPE_THETA ** (-jnp.arange(0, dim, 2, dtype=jnp.float32) / dim)
    ang = pos.astype(jnp.float32)[:, None] * inv[None, :]
    return jnp.cos(ang), jnp.sin(ang)

def apply_rope(x, cos, sin):
    half = x.shape[-1] // 2
    shp = (1, x.shape[1]) + (1,) * (x.ndim - 3) + (half,)
    c = cos.reshape(shp).astype(x.dtype)
    s = sin.reshape(shp).astype(x.dtype)
    x1, x2 = x[..., :half], x[..., half:]
    return jnp.concatenate([x1 * c - x2 * s, x1 * s + x2 * c], axis=-1)

def to_blocks(a):
    B, S = a.shape[:2]
    return jnp.moveaxis(a.reshape((B, S // Q_BLOCK, Q_BLOCK) + a.shape[2:]), 1, 0)

def from_blocks(o):
    o = jnp.moveaxis(o, 0, 1)
    return o.reshape((o.shape[0], o.shape[1] * o.shape[2]) + o.shape[3:])

def gqa_attention(q, k, v):
    scale = HEAD_DIM ** -0.5

    def block(qb):
        s = jnp.einsum('bqkgd,bskd->bkgqs', qb, k).astype(jnp.float32) * scale
        p = jax.nn.softmax(s, axis=-1).astype(v.dtype)
        return jnp.einsum('bkgqs,bskd->bqkgd', p, v)

    return from_blocks(lax.map(block, to_blocks(q)))

def diff_attention(q1, q2, k1, k2, v, lam):
    scale = HEAD_DIM ** -0.5

    def block(qs):
        q1b, q2b = qs
        s1 = jnp.einsum('bqhd,bshd->bhqs', q1b, k1).astype(jnp.float32) * scale
        s2 = jnp.einsum('bqhd,bshd->bhqs', q2b, k2).astype(jnp.float32) * scale
        p = (jax.nn.softmax(s1, axis=-1) - lam * jax.nn.softmax(s2, axis=-1)).astype(v.dtype)
        return jnp.einsum('bhqs,bshe->bqhe', p, v)

    return from_blocks(lax.map(block, (to_blocks(q1), to_blocks(q2))))

def encoder_layer(x, layer_idx, axial_cs, seq_cs, w_in, w_out, attn_norm, gqa_q_norm, gqa_k_norm,
                  lq1, lk1, lq2, lk2, diff_sub_norm, ffn_norm, w_gate_up, w_down):
    B, S, _ = x.shape
    (row_c, row_s, col_c, col_s) = axial_cs
    (t_c, t_s) = seq_cs
    h = rms_norm(x, attn_norm, NORM_EPS)
    proj = h @ w_in
    q_g, k_g, v_g, q_d, k_d, v_d = jnp.split(proj, SPLITS, axis=-1)

    q_g = rms_norm(q_g.reshape(B, S, GQA_HEADS, HEAD_DIM), gqa_q_norm, NORM_EPS)
    k_g = rms_norm(k_g.reshape(B, S, GQA_KV_HEADS, HEAD_DIM), gqa_k_norm, NORM_EPS)
    v_g = v_g.reshape(B, S, GQA_KV_HEADS, HEAD_DIM)

    def axial(a):
        return jnp.concatenate([apply_rope(a[..., :AXIAL_DIM], row_c, row_s),
                                apply_rope(a[..., AXIAL_DIM:], col_c, col_s)], axis=-1)

    q_g = axial(q_g).reshape(B, S, GQA_KV_HEADS, GQA_GROUP, HEAD_DIM)
    k_g = axial(k_g)
    o_g = gqa_attention(q_g, k_g, v_g).reshape(B, S, GQA_Q)

    q_d = apply_rope(q_d.reshape(B, S, DIFF_HEADS, 2, HEAD_DIM), t_c, t_s)
    k_d = apply_rope(k_d.reshape(B, S, DIFF_HEADS, 2, HEAD_DIM), t_c, t_s)
    v_d = v_d.reshape(B, S, DIFF_HEADS, DIFF_V_DIM)
    lambda_init = 0.8 - 0.6 * math.exp(-0.3 * layer_idx)
    lam = (jnp.exp(jnp.sum(lq1.astype(jnp.float32) * lk1.astype(jnp.float32)))
           - jnp.exp(jnp.sum(lq2.astype(jnp.float32) * lk2.astype(jnp.float32))) + lambda_init)
    o_d = diff_attention(q_d[..., 0, :], q_d[..., 1, :], k_d[..., 0, :], k_d[..., 1, :], v_d, lam)
    o_d = (rms_norm(o_d, diff_sub_norm, DIFF_NORM_EPS) * (1.0 - lambda_init)).reshape(B, S, DIFF_V)

    x = x + jnp.concatenate([o_g, o_d], axis=-1) @ w_out

    h = rms_norm(x, ffn_norm, NORM_EPS)
    gate, up = jnp.split(h @ w_gate_up, 2, axis=-1)
    return x + (jax.nn.silu(gate) * up) @ w_down

def encoder_trunk(x, w_in, w_out, attn_norm, gqa_q_norm, gqa_k_norm, diff_lambda_q1, diff_lambda_k1,
                  diff_lambda_q2, diff_lambda_k2, diff_sub_norm, ffn_norm, w_gate_up, w_down, final_norm):
    S = x.shape[1]
    rows = S // GRID_W
    row = jnp.repeat(jnp.arange(rows, dtype=jnp.int32), GRID_W)
    col = jnp.tile(jnp.arange(GRID_W, dtype=jnp.int32), rows)
    t = jnp.arange(S, dtype=jnp.int32)
    row_c, row_s = rope_angles(row, AXIAL_DIM)
    col_c, col_s = rope_angles(col, AXIAL_DIM)
    t_c, t_s = rope_angles(t, HEAD_DIM)
    for l in range(DEPTH):
        x = encoder_layer(x, l, (row_c, row_s, col_c, col_s), (t_c, t_s), w_in[l], w_out[l], attn_norm[l],
                          gqa_q_norm[l], gqa_k_norm[l], diff_lambda_q1[l], diff_lambda_k1[l],
                          diff_lambda_q2[l], diff_lambda_k2[l], diff_sub_norm[l], ffn_norm[l],
                          w_gate_up[l], w_down[l])
    return rms_norm(x, final_norm, NORM_EPS)

def setup_inputs(seed: int = 0) -> dict:
    key = jax.random.key(seed)
    ks = jax.random.split(key, 18)
    f32 = jnp.float32

    def gain(k, shape):
        return 1.0 + 0.02 * jax.random.normal(k, shape, f32)

    return {
        "x_prompt": jax.random.normal(ks[0], (BATCH, SEQ, D_MODEL), f32),
        "x_sample": jax.random.normal(ks[1], (DEC_BATCH, DEC_SEQ, D_MODEL), f32),
        "w_in": jax.random.normal(ks[2], (DEPTH, D_MODEL, IN_WIDTH), f32) * D_MODEL ** -0.5,
        "w_out": jax.random.normal(ks[3], (DEPTH, MIX_WIDTH, D_MODEL), f32) * MIX_WIDTH ** -0.5,
        "attn_norm": gain(ks[4], (DEPTH, D_MODEL)),
        "gqa_q_norm": gain(ks[5], (DEPTH, HEAD_DIM)),
        "gqa_k_norm": gain(ks[6], (DEPTH, HEAD_DIM)),
        "diff_lambda_q1": 0.1 * jax.random.normal(ks[7], (DEPTH, HEAD_DIM), f32),
        "diff_lambda_k1": 0.1 * jax.random.normal(ks[8], (DEPTH, HEAD_DIM), f32),
        "diff_lambda_q2": 0.1 * jax.random.normal(ks[9], (DEPTH, HEAD_DIM), f32),
        "diff_lambda_k2": 0.1 * jax.random.normal(ks[10], (DEPTH, HEAD_DIM), f32),
        "diff_sub_norm": gain(ks[11], (DEPTH, DIFF_V_DIM)),
        "ffn_norm": gain(ks[12], (DEPTH, D_MODEL)),
        "w_gate_up": jax.random.normal(ks[13], (DEPTH, D_MODEL, 2 * D_FF), f32) * D_MODEL ** -0.5,
        "w_down": jax.random.normal(ks[14], (DEPTH, D_FF, D_MODEL), f32) * D_FF ** -0.5,
        "final_norm": gain(ks[15], (D_MODEL,)),
    }

def reference(x_prompt, x_sample, w_in, w_out, attn_norm, gqa_q_norm, gqa_k_norm, diff_lambda_q1,
              diff_lambda_k1, diff_lambda_q2, diff_lambda_k2, diff_sub_norm, ffn_norm, w_gate_up, w_down,
              final_norm):
    y_prompt = encoder_trunk(x_prompt, w_in, w_out, attn_norm, gqa_q_norm, gqa_k_norm, diff_lambda_q1,
                             diff_lambda_k1, diff_lambda_q2, diff_lambda_k2, diff_sub_norm, ffn_norm,
                             w_gate_up, w_down, final_norm)
    y_sample = encoder_trunk(x_sample, w_in, w_out, attn_norm, gqa_q_norm, gqa_k_norm, diff_lambda_q1,
                             diff_lambda_k1, diff_lambda_q2, diff_lambda_k2, diff_sub_norm, ffn_norm,
                             w_gate_up, w_down, final_norm)
    return (y_prompt, y_sample)


_drawn_inputs = setup_inputs


def setup_inputs(seed=0):
    import zlib

    import numpy as np

    out = dict(_drawn_inputs(seed))
    spreads = {}
    factors = {'gqa_q_norm': 8.0,
     'gqa_k_norm': 8.0,
     'diff_lambda_q2': 4.136,
     'diff_sub_norm': 3.656,
     'ffn_norm': 3.2,
     'final_norm': 2.842}
    for name, (base, spread) in spreads.items():
        noise = np.random.default_rng([zlib.crc32(name.encode()), seed]).standard_normal(out[name].shape)
        drawn = base * np.exp(spread * noise) if base else spread * noise
        out[name] = __import__('jax').numpy.asarray(drawn.astype(out[name].dtype))
    for name, factor in factors.items():
        out[name] = (out[name] * factor).astype(out[name].dtype)
    return out
```

```python
import concourse.bass as bass
from concourse import mybir
from contextlib import ExitStack

F32 = mybir.dt.float32
F32R = mybir.dt.float32r
BF16 = mybir.dt.bfloat16
ALU = mybir.AluOpType
ACT = mybir.ActivationFunctionType
AX = mybir.AxisListType

P = 128
D = 1024
KT = D // P
T_PROMPT, T_SAMPLE = 2, 4
T = T_PROMPT + T_SAMPLE
TOK = T * P
HALF_TOK = TOK // 2
L = 2
HD = 64
GQA_Q, GQA_KV, DIFF_QK, DIFF_V = 512, 128, 512, 512
FF = 2816
FT = FF // P
EPS, SUB_EPS = 1e-6, 1e-5
PAIRS = 8
COLS = 512

PROJ = [(0, 512, 2, 8), (512, 256, 4, 2), (768, 512, 2, 8), (1280, 512, 2, 8), (1792, 512, 2, 0)]
FIRST_BLOCK = [0, 4, 6, 10]
N_BLOCKS = [4, 2, 4, 4]
FF_GROUPS = [8, 8, 6]

CHUNKS_IN = sum(KT // k for _, _, k, _ in PROJ)
CHUNKS_OUT = 2 * KT // 2
FFN_BASE = [CHUNKS_IN + CHUNKS_OUT + sum(3 * f for f in FF_GROUPS[:q]) for q in range(3)]
CHUNKS = CHUNKS_IN + CHUNKS_OUT + 3 * FT
RAW = 4
SPLIT = 2
assert CHUNKS % RAW == 0


def seq_of(t):
    return (0, T_PROMPT * P, t) if t < T_PROMPT else (T_PROMPT * P, T_SAMPLE * P, t - T_PROMPT)


def build(nc, x_prompt, x_sample, w_in, w_out, gqa_q_norm, gqa_k_norm, lq1, lk1, lq2, lk2,
          diff_sub_norm, gains, w_gate_up, w_down, ident_c, rope_c, laminit_c, y_prompt, y_sample):
    ctx = ExitStack()
    with ctx:
        def sb(name, shape, dt=F32, where=ctx):
            return where.enter_context(nc.sbuf_tensor(name, shape, dt))

        class Signal:
            def __init__(self, name, per, credit=0):
                self.sem = ctx.enter_context(nc.semaphore(name))
                self.per, self.credit = per, credit

            def at(self, l, k):
                return l * self.per + (self.credit + 1 + k)

        x = sb("x", [P, T, D])
        hT_hi = sb("hT_hi", [P, KT, TOK], F32R)
        hT_lo = sb("hT_lo", [P, KT, TOK], F32R)
        w_raw = [sb(f"w_raw{s}", [P, 1024]) for s in range(RAW)]
        w_hi = [sb(f"w_hi{s}", [P, 1024], F32R) for s in range(SPLIT)]
        w_lo = [sb(f"w_lo{s}", [P, 1024], F32R) for s in range(SPLIT)]
        stage = sb("stage", [P, T, COLS])
        h_row = stage[:, :, :].rearrange("p (s a) c -> p s (a c)", a=2)
        prob = stage[:, 0:4, :].rearrange("p (b h) c -> p b h c", h=2)
        probT = stage[:, 4:6, :].rearrange("p h (k q) -> p h k q", q=P)
        gain = sb("gain", [P, D])
        ident = sb("ident", [P, P])
        rope = sb("rope", [P, 4, 4, HD])
        rope_g = sb("rope_g", [P, 4, 4, HD])
        qk_gain = sb("qk_gain", [P, 2, L, HD])
        lam_in = stage[:, 5, :].rearrange("p (i l d) -> p i l d", i=4, l=L)
        lam_prod = stage[:, 4, 0:2 * L * HD].rearrange("p (s l d) -> p s l d", s=2, l=L)
        lam_sum = sb("lam_sum", [P, 2, L])
        lam_exp = sb("lam_exp", [P, 2, L])
        lam_dif = sb("lam_dif", [P, L])
        neg_lam = sb("neg_lam", [P, L])
        laminit = sb("laminit", [P, 2, L])
        neg_lam_l = sb("neg_lam_l", [P, 1])
        sub_all = sb("sub_all", [P, L, P])
        sub_gain = sb("sub_gain", [P, P])
        headsq = sb("headsq", [P, COLS])
        ss = sb("ss", [P, 1])
        ms = sb("ms", [P, 1])
        rstd = sb("rstd", [P, 1])
        hss = sb("hss", [P, 8])
        hms = sb("hms", [P, 8])
        hrstd = sb("hrstd", [P, 8])
        neg_half = sb("neg_half", [P, 8])
        eps_col = sb("eps_col", [P, 8])
        sub_eps = sb("sub_eps", [P, 1])
        neg_max = sb("neg_max", [P, 2, 2])
        row_sum = sb("row_sum", [P, 2, 2])
        inv_sum = sb("inv_sum", [P, 3, 2])
        neg_w2 = sb("neg_w2", [P, 1])
        oss = sb("oss", [P, 1])
        oms = sb("oms", [P, 1])
        orstd = sb("orstd", [P, 1])
        xn = sb("xn", [P, COLS])

        with ExitStack() as attn:
            qkT = sb("qkT", [P, 14, TOK], F32, attn)
            v = sb("v", [P, T, 640], F32, attn)
            q_hi = sb("q_hi", [P, TOK], F32R, attn)
            q_lo = sb("q_lo", [P, TOK], F32R, attn)
            k_hi = sb("k_hi", [P, TOK], F32R, attn)
            k_lo = sb("k_lo", [P, TOK], F32R, attn)
            mix = sb("mix", [P, T, P], F32, attn)
        with ExitStack() as ffn:
            actT_hi = sb("actT_hi", [P, max(FF_GROUPS), TOK], F32R, ffn)
            actT_lo = sb("actT_lo", [P, max(FF_GROUPS), TOK], F32R, ffn)
            silu = sb("silu", [P, 2, 2, HALF_TOK], F32, ffn)
        rope_t = mix[:, 0:4, :].rearrange("p a b -> p (a b)")

        bank = ctx.enter_context(nc.psum_tensor("bank", [P, 8, 512], F32))
        BANK_T = 6
        BANK_PT, BANK_O, BANK_M = 4, 6, 7

        const_loaded = Signal("const_loaded", 0)
        x_loaded = Signal("x_loaded", 0)
        gain_loaded = Signal("gain_loaded", 2)
        w_loaded = [Signal(f"w_loaded{s}", CHUNKS // RAW) for s in range(RAW)]
        w_hi_done = Signal("w_hi_done", CHUNKS)
        w_lo_done = Signal("w_lo_done", CHUNKS, credit=RAW)
        w_used = Signal("w_used", CHUNKS - 2 * FT - 13, credit=1)
        setup = Signal("setup", 0)
        half_set = Signal("half_set", 0)
        lam_exp_done = Signal("lam_exp_done", 0)
        x_added = Signal("x_added", 48, credit=T)
        ss_done = Signal("ss_done", 2 * T)
        ms_done = Signal("ms_done", 2 * T)
        rstd_done = Signal("rstd_done", 2 * T)
        h_ready = Signal("h_ready", 2 * T)
        h_tr = Signal("h_tr", 4 * T)
        hT_hi_done = Signal("hT_hi_done", 4 * T)
        hT_lo_done = Signal("hT_lo_done", 4 * T)
        layer_consts = Signal("layer_consts", 1)
        proj_done = Signal("proj_done", 5 * T)
        headsq_done = Signal("headsq_done", 2 * T)
        hss_done = Signal("hss_done", 2 * T)
        hms_done = Signal("hms_done", 2 * T)
        hrstd_done = Signal("hrstd_done", 2 * T)
        xn_done = Signal("xn_done", 2 * T)
        rope_s_done = Signal("rope_s_done", 2 * T)
        rope_t_done = Signal("rope_t_done", 4 * T)
        rot_ready = Signal("rot_ready", 4 * T)
        rot_tr = Signal("rot_tr", 4 * T)
        qkT_done = Signal("qkT_done", 4 * T)
        v_done = Signal("v_done", 2 * T)
        qk_hi_done = Signal("qk_hi_done", PAIRS)
        qk_split = Signal("qk_split", PAIRS)
        scores_done = Signal("scores_done", PAIRS * T)
        max_done = Signal("max_done", PAIRS * T)
        exp_done = Signal("exp_done", PAIRS * T, credit=2)
        inv_done = Signal("inv_done", PAIRS * T)
        w2_done = Signal("w2_done", 4 * T)
        p2_done = Signal("p2_done", 4 * T)
        p_comb = Signal("p_comb", 4 * T)
        pT_tr = Signal("pT_tr", PAIRS * T, credit=2)
        pT_act = Signal("pT_act", PAIRS * T)
        pT_dve = Signal("pT_dve", 4 * T)
        o_done = Signal("o_done", PAIRS * T, credit=1)
        oss_done = Signal("oss_done", 4 * T)
        oms_done = Signal("oms_done", 4 * T)
        orstd_done = Signal("orstd_done", 4 * T)
        mix_ready = Signal("mix_ready", PAIRS * T, credit=1)
        mix_tr = Signal("mix_tr", 2 * PAIRS)
        mixT_hi_done = Signal("mixT_hi_done", 2 * PAIRS)
        mixT_lo_done = Signal("mixT_lo_done", 2 * PAIRS, credit=1)
        out_done = Signal("out_done", 2 * T)
        gate_done = Signal("gate_done", FT)
        up_done = Signal("up_done", FT)
        silu_done = Signal("silu_done", FT)
        act_ready = Signal("act_ready", FT, credit=2)
        actT_hi_done = Signal("actT_hi_done", FT)
        actT_lo_done = Signal("actT_lo_done", FT, credit=2)
        down_done = Signal("down_done", 6 * T, credit=1)
        y_ready = Signal("y_ready", 0)
        y_stored = [Signal(f"y_stored{s}", 0) for s in range(3)]

        USED = {-2: (w_used, -1), -1: (down_done, -1)}
        for g, (_, _, k, _) in enumerate(PROJ):
            for kk in range(0, KT, k):
                USED[len(USED) - 2] = (proj_done, g * T + T - 1) if kk == KT - k else (w_used, None)
        for c in range(2):
            for kk in range(0, KT, 2):
                USED[len(USED) - 2] = (out_done, c * T + T - 1) if kk == KT - 2 else (w_used, None)
        f0 = 0
        for q, F in enumerate(FF_GROUPS):
            for f in range(f0, f0 + F):
                USED[len(USED) - 2] = (gate_done, f)
                USED[len(USED) - 2] = (up_done, f)
            for c in range(2):
                for kk in range(0, F, 2):
                    USED[len(USED) - 2] = (down_done, (2 * q + c) * T + T - 1) if kk == F - 2 else (w_used, None)
            f0 += F
        count = 0
        for n in range(CHUNKS):
            if USED[n][1] is None:
                USED[n] = (w_used, count)
                count += 1
        assert count == w_used.per

        block = ctx.enter_context(nc.Block())

        def spread(ap, axis, n):
            shape = list(ap.shape)
            return ap.unsqueeze(axis).broadcast_to(shape[:axis] + [n] + shape[axis:])

        def one(ap):
            return ap.rearrange("p o c -> p (o c)")

        def at(i, n=1):
            return bass.ds(i, n)

        win = w_in.rearrange("l (k p) c -> l p k c", p=P)
        wout = w_out.rearrange("l (k p) c -> l p k c", p=P)
        wgu = w_gate_up.rearrange("l (k p) c -> l p k c", p=P)
        wdn = w_down.rearrange("l (k p) c -> l p k c", p=P)

        @block.sync
        def _(sp):
            for t in range(T):
                src = x_prompt[0, t * P:(t + 1) * P, :] if t < T_PROMPT else \
                    x_sample[0, (t - T_PROMPT) * P:(t - T_PROMPT + 1) * P, :]
                sp.dma_start(x[:, t, :], src).then_inc(x_loaded.sem, 16)

            def load(l, n, slot, src, k, cols):
                sp.wait_ge(w_lo_done.sem, w_lo_done.at(l, n - RAW))
                sp.dma_start(w_raw[slot][:, :].rearrange("p (k c) -> p k c", k=k),
                             src.rearrange("l p k c -> (l p) k c")).then_inc(w_loaded[slot].sem, 16)

            with sp.Fori(0, L) as l:
                n = 0
                for c0, cols, k, _ in PROJ:
                    for kk in range(0, KT, k):
                        load(l, n, n % RAW, win[at(l), :, kk:kk + k, c0:c0 + cols], k, cols)
                        n += 1
                for c in range(2):
                    for kk in range(0, KT, 2):
                        load(l, n, n % RAW, wout[at(l), :, kk:kk + 2, c * COLS:(c + 1) * COLS], 2, COLS)
                        n += 1
                f0 = 0
                for q, F in enumerate(FF_GROUPS):
                    nb = FFN_BASE[q]
                    with sp.Fori(0, F // 2) as i:
                        for j in range(2):
                            for u in range(2):
                                m = nb + 2 * j + u
                                load(l, m + i * 4, m % RAW,
                                     wgu[at(l), :, :, at(i * (2 * P) + ((f0 + j) * P + u * FF), P)], KT, P)
                    for c in range(2):
                        for kk in range(0, F, 2):
                            m = nb + 2 * F + c * F // 2 + kk // 2
                            load(l, m, m % RAW, wdn[at(l), :, f0 + kk:f0 + kk + 2, c * COLS:(c + 1) * COLS], 2, COLS)
                    f0 += F

            for t in range(T):
                dst = y_prompt[0, t * P:(t + 1) * P, :] if t < T_PROMPT else \
                    y_sample[0, (t - T_PROMPT) * P:(t - T_PROMPT + 1) * P, :]
                sp.wait_ge(y_ready.sem, t + 1)
                sp.dma_start(dst, h_row[:, t % 3, :]).then_inc(y_stored[t % 3].sem, 16)
            for s in range(3):
                sp.wait_ge(y_stored[s].sem, 16 * T // 3)

        @block.gpsimd
        def _(pool):
            def row(ap):
                return ap.partition_broadcast(P)

            pool.dma_start(gain[:, :], row(gains[0, :])).then_inc(gain_loaded.sem, 16)
            pool.dma_start(ident[:, :], ident_c).then_inc(const_loaded.sem, 16)
            pool.dma_start(rope[:, :, :, :], rope_c).then_inc(const_loaded.sem, 16)
            pool.dma_start(laminit[:, :, :], laminit_c).then_inc(const_loaded.sem, 16)
            for i, src in enumerate((gqa_q_norm, gqa_k_norm)):
                pool.dma_start(qk_gain[:, i, :, :].rearrange("p l d -> p (l d)"),
                               row(src.rearrange("l d -> (l d)"))).then_inc(const_loaded.sem, 16)
            for i, src in enumerate((lq1, lk1, lq2, lk2)):
                pool.dma_start(lam_in[:, i, :, :].rearrange("p l d -> p (l d)"),
                               row(src.rearrange("l d -> (l d)"))).then_inc(const_loaded.sem, 16)
            pool.dma_start(sub_all[:, :, :].rearrange("p l d -> p (l d)"),
                           row(diff_sub_norm.rearrange("l d -> (l d)"))).then_inc(const_loaded.sem, 16)
            pool.memset(neg_half[:, :], -0.5).then_inc(half_set.sem, 1)
            pool.memset(eps_col[:, :], EPS).then_inc(half_set.sem, 1)
            pool.memset(sub_eps[:, :], 2 * SUB_EPS).then_inc(half_set.sem, 1)

            def inverse_rms(l, e, sums, sums_ready, mean, mean_ready, out, out_ready, eps, used, used_event):
                if used is not None:
                    pool.wait_ge(used.sem, used.at(l, used_event))
                pool.wait_ge(sums_ready.sem, sums_ready.at(l, e))
                pool.tensor_tensor(mean, sums, eps, ALU.add).then_inc(mean_ready.sem, 1)
                pool.wait_ge(mean_ready.sem, mean_ready.at(l, e))
                pool.tensor_tensor(out, mean, neg_half[:, 0:out.shape[1]], ALU.pow).then_inc(out_ready.sem, 1)

            def norm(l, m):
                for t in range(T):
                    e = m * T + t
                    inverse_rms(l, e, ss[:, :], ss_done, ms[:, :], ms_done, rstd[:, :], rstd_done, eps_col[:, 0:1],
                                h_ready if e else None, e - 1)

            pool.wait_ge(half_set.sem, 3)
            with pool.Fori(0, L) as l:
                norm(l, 0)
                pool.wait_ge(h_ready.sem, h_ready.at(l, T - 1))
                pool.dma_start(gain[:, :], row(gains[at(l * 2 + 1), :].rearrange("o c -> (o c)"))).then_inc(gain_loaded.sem, 16)
                for g in range(2):
                    heads = PROJ[g][3]
                    for t in range(T):
                        e = g * T + t
                        inverse_rms(l, e, hss[:, 0:heads], hss_done, hms[:, 0:heads], hms_done, hrstd[:, 0:heads],
                                    hrstd_done, eps_col[:, 0:heads], xn_done if e else None, e - 1)
                with pool.Fori(0, 4) as h:
                    for t in range(T):
                        inverse_rms(l, h * T + t, oss[:, :], oss_done, oms[:, :], oms_done, orstd[:, :], orstd_done,
                                    sub_eps[:, :], mix_ready, h * T + (4 * T + t - 1))
                norm(l, 1)
                pool.wait_ge(h_ready.sem, h_ready.at(l, 2 * T - 1))
                pool.dma_start(gain[:, :], row(gains[at(l * 2 + 2), :].rearrange("o c -> (o c)"))).then_inc(gain_loaded.sem, 16)
            for t in range(T):
                if t:
                    pool.wait_ge(y_ready.sem, t)
                inverse_rms(L, t, ss[:, :], ss_done, ms[:, :], ms_done, rstd[:, :], rstd_done, eps_col[:, 0:1], None, None)

        @block.scalar
        def _(act):
            def high(l, n0, turn, used, event):
                act.wait_ge(w_loaded[n0 % RAW].sem, (l * (CHUNKS // RAW) + (turn + 1)) * 16)
                act.wait_ge(used.sem, used.at(l, event))
                act.activation(w_hi[n0 % SPLIT][:, :], w_raw[n0 % RAW][:, :], ACT.Copy).then_inc(w_hi_done.sem, 1)

            def high_at(l, n):
                high(l, n, n // RAW, *USED[n - SPLIT])

            act.wait_ge(setup.sem, 2)
            act.activation(lam_exp[:, :, :], lam_sum[:, :, :], ACT.Exp).then_inc(lam_exp_done.sem, 1)

            def norm(l, m):
                for t in range(T + 1):
                    if t < T:
                        act.wait_ge(x_added.sem, x_added.at(l, (-T if m == 0 else T) + t))
                        act.wait_ge(ms_done.sem, ms_done.at(l, m * T + t - 1)) if m or t else None
                        act.activation(headsq[:, :].bitcast(BF16), x[:, t, :], ACT.Square,
                                       scale=D ** -0.5, accum_out=ss[:, :]).then_inc(ss_done.sem, 1)
                    if t:
                        for b in range(2):
                            e = 2 * (m * T + t - 1) + b
                            act.wait_ge(h_tr.sem, h_tr.at(l, e))
                            act.activation(hT_hi[:, 4 * b:4 * b + 4, (t - 1) * P:t * P],
                                           bank[:, BANK_T + b, :].rearrange("p (k q) -> p k q", q=P),
                                           ACT.Copy).then_inc(hT_hi_done.sem, 1)

            def copy_qkT(l, g, t):
                e = g * T + t
                act.wait_ge(rot_tr.sem, rot_tr.at(l, e))
                nb, b0 = N_BLOCKS[g], FIRST_BLOCK[g]
                act.activation(qkT[:, b0:b0 + nb, t * P:(t + 1) * P],
                               bank[:, BANK_T + t % 2, 0:nb * P].rearrange("p (k q) -> p k q", q=P),
                               ACT.Copy).then_inc(qkT_done.sem, 1)

            def read_projection(l, g, t, heads):
                e = g * T + t
                if g == 2 or g == 3:
                    return
                act.wait_ge(proj_done.sem, proj_done.at(l, e))
                if g == 4:
                    act.activation(v[:, t, P:P + DIFF_V], bank[:, t, :], ACT.Copy).then_inc(v_done.sem, 1)
                    return
                if g == 1:
                    act.activation(v[:, t, 0:P], bank[:, t, P:2 * P], ACT.Copy).then_inc(v_done.sem, 1)
                if e:
                    act.wait_ge(hss_done.sem, hss_done.at(l, e - 1))
                act.activation(headsq[:, 0:heads * HD], bank[:, t, 0:heads * HD],
                               ACT.Square, scale=HD ** -0.5).then_inc(headsq_done.sem, 1)

            def exps(l, e, t):
                S = seq_of(t)[1]
                b = t % 2
                act.wait_ge(max_done.sem, max_done.at(l, e))
                act.wait_ge(pT_tr.sem, pT_tr.at(l, e - 2))
                act.activation(prob[:, b, 0, 0:S], bank[:, 2 * b, 0:S], ACT.Exp, bias=neg_max[:, b, 0:1],
                               accum_out=row_sum[:, b, 0:1])
                act.activation(prob[:, b, 1, 0:S], bank[:, 2 * b + 1, 0:S], ACT.Exp, bias=neg_max[:, b, 1:2],
                               accum_out=row_sum[:, b, 1:2]).then_inc(exp_done.sem, 1)

            def mixT_high(l, p, e, part):
                t0, n = (0, 2) if part == 0 else (2, 4)
                act.wait_ge(mix_tr.sem, mix_tr.at(l, 2 * e + part))
                act.activation(one(hT_hi[:, at(p), t0 * P:(t0 + n) * P]), bank[:, BANK_M, 0:n * P],
                               ACT.Copy).then_inc(mixT_hi_done.sem, 1)

            def pair(l, p, e0, gqa, qb, kb):
                act.activation(q_hi[:, :], one(qkT[:, at(qb), :]), ACT.Copy, scale=HD ** -0.5)
                act.activation(k_hi[:, :], one(qkT[:, at(kb), :]), ACT.Copy).then_inc(qk_hi_done.sem, 1)
                exps(l, e0, 0)
                exps(l, e0 + 1, 1)
                for t in range(T + 1):
                    if t < T:
                        nk = seq_of(t)[1] // P
                        act.wait_ge(pT_tr.sem, pT_tr.at(l, e0 + t))
                        act.wait_ge(o_done.sem, o_done.at(l, e0 + t - 1))
                        if gqa:
                            src, dst = bank[:, BANK_PT, 0:nk * P], probT[:, 0, 0:nk, :]
                        else:
                            src, dst = bank[:, BANK_PT + t % 2, 0:nk * P], probT[:, t % 2, 0:nk, :]
                        act.activation(dst, src.rearrange("p (k q) -> p k q", q=P), ACT.Copy).then_inc(pT_act.sem, 1)
                    if not gqa and t:
                        act.wait_ge(o_done.sem, o_done.at(l, e0 + t - 1))
                        act.wait_ge(mix_ready.sem, mix_ready.at(l, e0 + t - 2))
                        act.activation(headsq[:, 0:P], bank[:, BANK_O, 0:P], ACT.Square, scale=1 / 8,
                                       accum_out=oss[:, :]).then_inc(oss_done.sem, 1)
                    if t + 2 < T:
                        exps(l, e0 + t + 2, t + 2)
                    if t == 3:
                        mixT_high(l, p, p, 0)
                mixT_high(l, p, p, 1)

            with act.Fori(0, L) as l:
                high_at(l, 0)
                high_at(l, 1)
                norm(l, 0)
                n = 0
                for g, (c0, cols, k, heads) in enumerate(PROJ):
                    for kk in range(0, KT, k):
                        if kk == 0 and g:
                            for t in range(T):
                                copy_qkT(l, g - 1, t)
                        last = kk == KT - k
                        for t in range(T):
                            if t == 3 and last:
                                high_at(l, n + 2)
                            if last:
                                read_projection(l, g, t, heads)
                        if not last:
                            high_at(l, n + 2)
                        n += 1
                act.wait_ge(qkT_done.sem, qkT_done.at(l, 4 * T - 1))
                with act.Fori(0, 2) as kv:
                    with act.Fori(0, 2) as r:
                        p = kv * 2 + r
                        pair(l, p, kv * (2 * T) + r * T, True, p, kv + 4)
                with act.Fori(0, 4) as h:
                    pair(l, h + 4, h * T + 4 * T, False, h + 6, h + 10)
                for _ in range(CHUNKS_OUT):
                    high_at(l, n + 2)
                    n += 1
                norm(l, 1)
                f0 = 0
                for q, F in enumerate(FF_GROUPS):
                    nb = FFN_BASE[q]
                    with act.Fori(0, F // 2) as i:
                        for j in range(2):
                            e = i * 2 + (f0 + j)
                            act.wait_ge(gate_done.sem, gate_done.at(l, e))
                            act.wait_ge(actT_lo_done.sem, actT_lo_done.at(l, e - 2))
                            act.activation(silu[:, j, :, :], bank[:, 4 * j:4 * j + 2, 0:HALF_TOK],
                                           ACT.Silu).then_inc(silu_done.sem, 1)
                            m = nb + 2 * j + 2
                            high(l, m, i + m // RAW, gate_done, e)
                            act.wait_ge(act_ready.sem, act_ready.at(l, e))
                            act.activation(one(actT_hi[:, at(i * 2 + j), :]),
                                           silu[:, j, :, :].rearrange("p a b -> p (a b)"),
                                           ACT.Copy).then_inc(actT_hi_done.sem, 1)
                            high(l, m + 1, i + (m + 1) // RAW, up_done, e)
                    for m in range(nb + 2 * F, nb + 3 * F):
                        if m + 2 < CHUNKS:
                            high_at(l, m + 2)
                    f0 += F
            for t in range(T):
                act.wait_ge(x_added.sem, x_added.at(L, -T + t))
                act.wait_ge(ms_done.sem, ms_done.at(L, t - 1))
                act.activation(headsq[:, :].bitcast(BF16), x[:, t, :], ACT.Square,
                               scale=D ** -0.5, accum_out=ss[:, :]).then_inc(ss_done.sem, 1)

        @block.vector
        def _(dve):
            def low(l, n0, n):
                dve.wait_ge(w_hi_done.sem, w_hi_done.at(l, n))
                dve.tensor_tensor(w_lo[n0 % SPLIT][:, :], w_raw[n0 % RAW][:, :], w_hi[n0 % SPLIT][:, :].bitcast(F32),
                                  ALU.subtract).then_inc(w_lo_done.sem, 1)

            def norm(l, m):
                dve.wait_ge(gain_loaded.sem, (l * 2 + (m + 1)) * 16)
                for t in range(T + 1):
                    if t < T:
                        e = m * T + t
                        dve.wait_ge(rstd_done.sem, rstd_done.at(l, e))
                        if t >= 3:
                            dve.wait_ge(h_tr.sem, h_tr.at(l, 2 * (e - 3) + 1))
                        dve.scalar_tensor_tensor(h_row[:, t % 3, :], x[:, t, :], rstd[:, :], gain[:, :], ALU.mult,
                                                 ALU.mult).then_inc(h_ready.sem, 1)
                    if t:
                        for b in range(2):
                            e = 2 * (m * T + t - 1) + b
                            dve.wait_ge(hT_hi_done.sem, hT_hi_done.at(l, e))
                            dst = (slice(None), slice(4 * b, 4 * b + 4), slice((t - 1) * P, t * P))
                            dve.tensor_tensor(hT_lo[dst], bank[:, BANK_T + b, :].rearrange("p (k q) -> p k q", q=P),
                                              hT_hi[dst].bitcast(F32), ALU.subtract).then_inc(hT_lo_done.sem, 1)

            def rotate(l, g, t, heads):
                e = g * T + t
                pos = seq_of(t)[2]
                W = heads * HD
                dve.wait_ge(proj_done.sem, proj_done.at(l, e))
                if g < 2:
                    dve.wait_ge(headsq_done.sem, headsq_done.at(l, e))
                    dve.tensor_reduce(hss[:, 0:heads], headsq[:, 0:W].rearrange("p (h d) -> p h d", d=HD), AX.X,
                                      ALU.add).then_inc(hss_done.sem, 1)
                    dve.wait_ge(hrstd_done.sem, hrstd_done.at(l, e))
                    if g == 1:
                        dve.wait_ge(v_done.sem, v_done.at(l, t))
                    if e:
                        dve.wait_ge(rot_ready.sem, rot_ready.at(l, e - 1))
                    dve.tensor_tensor(xn[:, 0:W].rearrange("p (h d) -> p h d", d=HD),
                                      bank[:, t, 0:W].rearrange("p (h d) -> p h d", d=HD),
                                      spread(hrstd[:, 0:heads], 2, HD), ALU.mult).then_inc(xn_done.sem, 1)
                    dve.wait_ge(xn_done.sem, xn_done.at(l, e))
                    src = xn[:, 0:W]
                    cos, sin = rope_g[:, 2 * g, pos, :], rope_g[:, 2 * g + 1, pos, :]
                    groups, half = 2, HD // 4
                else:
                    src = bank[:, t, :]
                    cos, sin = rope[:, 0, pos, :], rope[:, 1, pos, :]
                    groups, half = 1, HD // 2
                if e and g >= 2:
                    dve.wait_ge(rot_ready.sem, rot_ready.at(l, e - 1))
                for a in range(2):
                    last = dve.tensor_tensor(
                        rope_t[:, 0:W].rearrange("p (h r a d) -> p h r a d", r=groups, a=2, d=half)[:, :, :, a, :],
                        src.rearrange("p (h r a d) -> p h r a d", r=groups, a=2, d=half)[:, :, :, 1 - a, :],
                        spread(sin.rearrange("p (r a d) -> p r a d", r=groups, a=2)[:, :, a, :], 1, heads), ALU.mult)
                if g < 2:
                    last.then_inc(rope_s_done.sem, 1)
                    dve.wait_ge(rope_s_done.sem, rope_s_done.at(l, e))
                dve.tensor_tensor(xn[:, 0:W].rearrange("p (h d) -> p h d", d=HD),
                                  src.rearrange("p (h d) -> p h d", d=HD), spread(cos, 1, heads),
                                  ALU.mult).then_inc(rope_t_done.sem, 1)
                dve.wait_ge(rope_t_done.sem, rope_t_done.at(l, e))
                if e >= T:
                    dve.wait_ge(rot_tr.sem, rot_tr.at(l, e - T))
                if g == 1:
                    dve.tensor_tensor(stage[:, t, 0:2 * W].rearrange("p (h r d) -> p h r d", r=2, d=HD),
                                      spread(xn[:, 0:W].rearrange("p (h d) -> p h d", d=HD), 2, 2),
                                      spread(rope_t[:, 0:W].rearrange("p (h d) -> p h d", d=HD), 2, 2),
                                      ALU.add).then_inc(rot_ready.sem, 1)
                else:
                    dve.tensor_tensor(stage[:, t, :], xn[:, :], rope_t[:, :], ALU.add).then_inc(rot_ready.sem, 1)

            def row_max(l, e, t):
                S = seq_of(t)[1]
                b = t % 2
                dve.wait_ge(scores_done.sem, scores_done.at(l, e))
                dve.tensor_reduce(neg_max[:, b, :], bank[:, 2 * b:2 * b + 2, 0:S], AX.X, ALU.max,
                                  negate=True).then_inc(max_done.sem, 1)

            def combine(l, e, ed, t, gqa):
                S = seq_of(t)[1]
                b = t % 2
                dve.wait_ge(exp_done.sem, exp_done.at(l, e))
                dve.reciprocal(inv_sum[:, t % 3, :], row_sum[:, b, :]).then_inc(inv_done.sem, 1)
                if gqa:
                    return
                dve.wait_ge(inv_done.sem, inv_done.at(l, e))
                dve.tensor_tensor(neg_w2[:, :], inv_sum[:, t % 3, 1:2], neg_lam_l[:, :], ALU.mult).then_inc(w2_done.sem, 1)
                dve.wait_ge(w2_done.sem, w2_done.at(l, ed))
                dve.tensor_scalar(prob[:, b, 1, 0:S], prob[:, b, 1, 0:S], neg_w2[:, :], None,
                                  ALU.mult).then_inc(p2_done.sem, 1)
                dve.wait_ge(p2_done.sem, p2_done.at(l, ed))
                dve.scalar_tensor_tensor(prob[:, b, 0, 0:S], prob[:, b, 0, 0:S], inv_sum[:, t % 3, 0:1],
                                         prob[:, b, 1, 0:S], ALU.mult, ALU.add).then_inc(p_comb.sem, 1)

            def mixT_low(l, p, part):
                t0, n = (0, 2) if part == 0 else (2, 4)
                dve.wait_ge(mixT_hi_done.sem, mixT_hi_done.at(l, 2 * p + part))
                dve.tensor_tensor(one(hT_lo[:, at(p), t0 * P:(t0 + n) * P]), bank[:, BANK_M, 0:n * P],
                                  one(hT_hi[:, at(p), t0 * P:(t0 + n) * P]).bitcast(F32),
                                  ALU.subtract).then_inc(mixT_lo_done.sem, 1)

            def pair(l, p, e0, ed0, gqa, qb, kb):
                dve.wait_ge(qk_hi_done.sem, qk_hi_done.at(l, p))
                dve.scalar_tensor_tensor(q_lo[:, :], one(qkT[:, at(qb), :]), HD ** -0.5, q_hi[:, :].bitcast(F32),
                                         ALU.mult, ALU.subtract)
                dve.tensor_tensor(k_lo[:, :], one(qkT[:, at(kb), :]), k_hi[:, :].bitcast(F32),
                                  ALU.subtract).then_inc(qk_split.sem, 1)
                row_max(l, e0, 0)
                row_max(l, e0 + 1, 1)
                combine(l, e0, ed0, 0, gqa)
                for t in range(T + 1):
                    if t + 1 < T:
                        combine(l, e0 + t + 1, ed0 + t + 1, t + 1, gqa)
                    if gqa and t < T:
                        nk = seq_of(t)[1] // P
                        dve.wait_ge(pT_tr.sem, pT_tr.at(l, e0 + t))
                        dve.wait_ge(o_done.sem, o_done.at(l, e0 + t - 1))
                        dve.tensor_copy(probT[:, 1, 0:nk, :], bank[:, BANK_PT + 1, 0:nk * P].rearrange(
                            "p (k q) -> p k q", q=P)).then_inc(pT_dve.sem, 1)
                    if t:
                        u = t - 1
                        e = e0 + u
                        if gqa:
                            dve.wait_ge(o_done.sem, o_done.at(l, e))
                            dve.wait_ge(inv_done.sem, inv_done.at(l, e))
                            dve.tensor_tensor(mix[:, u, :].rearrange("p (h d) -> p h d", d=HD),
                                              bank[:, BANK_O, 0:P].rearrange("p (h d) -> p h d", d=HD),
                                              spread(inv_sum[:, u % 3, :], 2, HD), ALU.mult).then_inc(mix_ready.sem, 1)
                        else:
                            dve.wait_ge(orstd_done.sem, orstd_done.at(l, ed0 + u))
                            dve.scalar_tensor_tensor(mix[:, u, :], bank[:, BANK_O, 0:P], orstd[:, :], sub_gain[:, :],
                                                     ALU.mult, ALU.mult).then_inc(mix_ready.sem, 1)
                    if t + 2 < T:
                        row_max(l, e0 + t + 2, t + 2)
                    if t == 3:
                        mixT_low(l, p, 0)
                mixT_low(l, p, 1)

            def add_to_x(l, e, done, ed, t, c):
                dve.wait_ge(done.sem, done.at(l, ed))
                xs = x[:, t, c * COLS:(c + 1) * COLS]
                dve.tensor_tensor(xs, xs, bank[:, t, :], ALU.add).then_inc(x_added.sem, 1)

            dve.sem_inc(w_lo_done.sem, RAW)
            dve.sem_inc(w_used.sem, 1)
            dve.sem_inc(down_done.sem, 1)
            dve.sem_inc(exp_done.sem, 2)
            dve.sem_inc(pT_tr.sem, 2)
            dve.sem_inc(o_done.sem, 1)
            dve.sem_inc(mix_ready.sem, 1)
            dve.sem_inc(mixT_lo_done.sem, 1)
            dve.sem_inc(act_ready.sem, 2)
            dve.sem_inc(actT_lo_done.sem, 2)
            dve.wait_ge(x_loaded.sem, 16 * T)
            dve.sem_inc(x_added.sem, T)
            dve.wait_ge(const_loaded.sem, 16 * 10)
            pairs = lam_in[:, :, :, :].rearrange("p (s a) l d -> p s a (l d)", a=2)
            dve.tensor_tensor(lam_prod[:, :, :, :].rearrange("p s l d -> p s (l d)"), pairs[:, :, 0, :], pairs[:, :, 1, :],
                              ALU.mult).then_inc(setup.sem, 1)
            dve.wait_ge(setup.sem, 1)
            dve.tensor_reduce(lam_sum[:, :, :], lam_prod[:, :, :, :], AX.X, ALU.add).then_inc(setup.sem, 1)
            dve.wait_ge(lam_exp_done.sem, 1)
            dve.tensor_tensor(lam_dif[:, :], lam_exp[:, 1, :], lam_exp[:, 0, :], ALU.subtract).then_inc(setup.sem, 1)
            dve.wait_ge(setup.sem, 3)
            dve.tensor_tensor(neg_lam[:, :], lam_dif[:, :], laminit[:, 0, :], ALU.subtract).then_inc(setup.sem, 1)
            dve.wait_ge(setup.sem, 4)

            with dve.Fori(0, L) as l:
                dve.tensor_copy(neg_lam_l[:, :], neg_lam[:, at(l)])
                dve.tensor_tensor(sub_gain[:, :], one(sub_all[:, at(l), :]), laminit[:, 1, at(l)].broadcast_to([P, P]),
                                  ALU.mult)
                for i in range(2):
                    g = one(qk_gain[:, i, at(l), :])
                    dve.tensor_tensor(rope_g[:, 2 * i, :, :], rope[:, 2, :, :], spread(g, 1, 4), ALU.mult)
                    for a in range(2):
                        def part(ap, which):
                            return ap.rearrange("p t (r a d) -> p t r a d", r=2, a=2)[:, :, :, which, :]
                        gs = g.rearrange("p (r a d) -> p r a d", r=2, a=2)[:, :, 1 - a, :]
                        last = dve.tensor_tensor(part(rope_g[:, 2 * i + 1, :, :], a), part(rope[:, 3, :, :], a),
                                                 spread(gs, 1, 4), ALU.mult)
                last.then_inc(layer_consts.sem, 1)
                dve.wait_ge(layer_consts.sem, layer_consts.at(l, 0))
                low(l, 0, 0)
                low(l, 1, 1)
                norm(l, 0)
                n = 0
                for g, (c0, cols, k, heads) in enumerate(PROJ):
                    for kk in range(0, KT, k):
                        last = kk == KT - k and g < 4
                        for t in range(3 if last else 0):
                            rotate(l, g, t, heads)
                        low(l, n + 2, n + 2)
                        for t in range(3 if last else T, T):
                            rotate(l, g, t, heads)
                        n += 1
                with dve.Fori(0, 2) as kv:
                    with dve.Fori(0, 2) as r:
                        p = kv * 2 + r
                        pair(l, p, kv * (2 * T) + r * T, 0, True, p, kv + 4)
                with dve.Fori(0, 4) as h:
                    pair(l, h + 4, h * T + 4 * T, h * T, False, h + 6, h + 10)
                for c in range(2):
                    for kk in range(0, KT, 2):
                        if kk == KT - 2:
                            for t in range(T):
                                add_to_x(l, None, out_done, c * T + t, t, c)
                        low(l, n + 2, n + 2)
                        n += 1
                norm(l, 1)
                f0 = 0
                for q, F in enumerate(FF_GROUPS):
                    nb = FFN_BASE[q]
                    with dve.Fori(0, F // 2) as i:
                        for j in range(2):
                            e = i * 2 + (f0 + j)
                            m = nb + 2 * j + 2
                            low(l, m, m + i * 4)
                            dve.wait_ge(up_done.sem, up_done.at(l, e))
                            dve.wait_ge(silu_done.sem, silu_done.at(l, e))
                            s = silu[:, j, :, :]
                            dve.tensor_tensor(s, s, bank[:, 4 * j + 2:4 * j + 4, 0:HALF_TOK],
                                              ALU.mult).then_inc(act_ready.sem, 1)
                            dve.wait_ge(actT_hi_done.sem, actT_hi_done.at(l, e))
                            dst = at(i * 2 + j)
                            dve.tensor_tensor(one(actT_lo[:, dst, :]), silu[:, j, :, :].rearrange("p a b -> p (a b)"),
                                              one(actT_hi[:, dst, :]).bitcast(F32),
                                              ALU.subtract).then_inc(actT_lo_done.sem, 1)
                            low(l, m + 1, m + 1 + i * 4)
                    for c in range(2):
                        for kk in range(0, F, 2):
                            m = nb + 2 * F + c * F // 2 + kk // 2
                            if kk == F - 2:
                                for t in range(T):
                                    add_to_x(l, None, down_done, (2 * q + c) * T + t, t, c)
                            if m + 2 < CHUNKS:
                                low(l, m + 2, m + 2)
                    f0 += F
            dve.wait_ge(gain_loaded.sem, (2 * L + 1) * 16)
            for t in range(T):
                dve.wait_ge(rstd_done.sem, rstd_done.at(L, t))
                if t >= 3:
                    dve.wait_ge(y_stored[t % 3].sem, 16)
                dve.scalar_tensor_tensor(h_row[:, t % 3, :], x[:, t, :], rstd[:, :], gain[:, :], ALU.mult,
                                         ALU.mult).then_inc(y_ready.sem, 1)

        @block.tensor
        def _(pe):
            def mm3(out, a_hi, a_lo, b_hi, b_lo, first, last):
                pe.matmul(out, a_hi, b_hi, start=first, stop=False)
                pe.matmul(out, a_hi, b_lo, start=False, stop=False)
                return pe.matmul(out, a_lo, b_hi, start=False, stop=last)

            def chunk(n0, k):
                s = n0 % SPLIT
                return (w_hi[s][:, :].rearrange("p (k c) -> p k c", k=k),
                        w_lo[s][:, :].rearrange("p (k c) -> p k c", k=k))

            def transpose_rows(l, m, t):
                e = m * T + t
                pe.wait_ge(h_ready.sem, h_ready.at(l, e))
                for b in range(2):
                    if e:
                        pe.wait_ge(hT_lo_done.sem, hT_lo_done.at(l, 2 * e + b - 2))
                    for k in range(4):
                        last = pe.transpose(bank[:, BANK_T + b, k * P:(k + 1) * P],
                                            h_row[:, t % 3, (4 * b + k) * P:(4 * b + k + 1) * P], ident[:, :])
                    last.then_inc(h_tr.sem, 1)

            def rows_product(l, t, n0, k, kt0, cols, srcT, first, last):
                hi, lo = chunk(n0, k)
                a_hi, a_lo = srcT
                for kk in range(k):
                    i = mm3(bank[:, t, 0:cols], a_hi[:, kt0 + kk, t * P:(t + 1) * P], a_lo[:, kt0 + kk, t * P:(t + 1) * P],
                            hi[:, kk, :], lo[:, kk, :], first and kk == 0, last and kk == k - 1)
                return i

            def scores(l, e, t, p):
                k0, S, _ = seq_of(t)
                b = t % 2
                pe.wait_ge(exp_done.sem, exp_done.at(l, e - 2))
                for h in range(2):
                    rows = slice(h * HD, (h + 1) * HD)
                    i = mm3(bank[:, 2 * b + h, 0:S], q_hi[rows, t * P:(t + 1) * P], q_lo[rows, t * P:(t + 1) * P],
                            k_hi[rows, k0:k0 + S], k_lo[rows, k0:k0 + S], True, True)
                i.then_inc(scores_done.sem, 1)

            def transpose_mix(l, p, e0, part):
                t0, n = (0, 2) if part == 0 else (2, 4)
                pe.wait_ge(mix_ready.sem, mix_ready.at(l, e0 + t0 + n - 1))
                pe.wait_ge(mixT_lo_done.sem, mixT_lo_done.at(l, 2 * p + part - 1))
                for t in range(n):
                    last = pe.transpose(bank[:, BANK_M, t * P:(t + 1) * P], mix[:, t0 + t, :], ident[:, :])
                last.then_inc(mix_tr.sem, 1)

            def pair(l, p, e0, ed0, gqa, vcol):
                pe.wait_ge(v_done.sem, v_done.at(l, 2 * T - 1))
                pe.wait_ge(qk_split.sem, qk_split.at(l, p))
                scores(l, e0, 0, p)
                scores(l, e0 + 1, 1, p)
                for t in range(T + 1):
                    if t + 2 < T:
                        scores(l, e0 + t + 2, t + 2, p)
                    if t < T:
                        e = e0 + t
                        b = t % 2
                        nk = seq_of(t)[1] // P
                        if gqa:
                            pe.wait_ge(exp_done.sem, exp_done.at(l, e))
                            if t:
                                pe.wait_ge(pT_act.sem, pT_act.at(l, e - 1))
                                pe.wait_ge(pT_dve.sem, pT_dve.at(l, e - 1))
                        else:
                            pe.wait_ge(p_comb.sem, p_comb.at(l, ed0 + t))
                            if t >= 2:
                                pe.wait_ge(pT_act.sem, pT_act.at(l, e - 2))
                        for h in range(2 if gqa else 1):
                            dst = BANK_PT + (h if gqa else b)
                            for k in range(nk):
                                last = pe.transpose(bank[:, dst, k * P:(k + 1) * P],
                                                    prob[:, b, h, k * P:(k + 1) * P], ident[:, :])
                        last.then_inc(pT_tr.sem, 1)
                    if t:
                        u = t - 1
                        e = e0 + u
                        k0, S, _ = seq_of(u)
                        nk, kt0 = S // P, k0 // P
                        pe.wait_ge(pT_act.sem, pT_act.at(l, e))
                        pe.wait_ge(mix_ready.sem, mix_ready.at(l, e - 1))
                        if gqa:
                            pe.wait_ge(pT_dve.sem, pT_dve.at(l, e))
                            for h in range(2):
                                for k in range(nk):
                                    last = pe.matmul(bank[:, BANK_O, h * HD:(h + 1) * HD], probT[:, h, k, :],
                                                     v[:, kt0 + k, at(vcol, HD)], start=k == 0, stop=k == nk - 1)
                        else:
                            for k in range(nk):
                                last = pe.matmul(bank[:, BANK_O, 0:P], probT[:, u % 2, k, :],
                                                 v[:, kt0 + k, at(vcol, P)], start=k == 0, stop=k == nk - 1)
                        last.then_inc(o_done.sem, 1)
                    if t == 3:
                        transpose_mix(l, p, e0, 0)
                transpose_mix(l, p, e0, 1)

            hT = (hT_hi, hT_lo)
            actT = (actT_hi, actT_lo)
            pe.wait_ge(const_loaded.sem, 16 * 10)
            with pe.Fori(0, L) as l:
                n = 0
                transpose_rows(l, 0, 0)
                for g, (c0, cols, k, heads) in enumerate(PROJ):
                    for kk in range(0, KT, k):
                        pe.wait_ge(w_lo_done.sem, w_lo_done.at(l, n))
                        for t in range(T):
                            if n == 0:
                                if t + 1 < T:
                                    transpose_rows(l, 0, t + 1)
                                pe.wait_ge(hT_lo_done.sem, hT_lo_done.at(l, 2 * t + 1))
                            if kk == 0 and g:
                                pe.wait_ge(rope_t_done.sem, rope_t_done.at(l, (g - 1) * T + t))
                            i = rows_product(l, t, n, k, kk, cols, hT, kk == 0, kk == KT - k)
                            if kk == KT - k:
                                i.then_inc(proj_done.sem, 1)
                            elif t == T - 1:
                                i.then_inc(w_used.sem, 1)
                            if kk == 0 and g:
                                e = (g - 1) * T + t
                                pe.wait_ge(rot_ready.sem, rot_ready.at(l, e))
                                if e >= 2:
                                    pe.wait_ge(qkT_done.sem, qkT_done.at(l, e - 2))
                                for b in range(N_BLOCKS[g - 1]):
                                    last = pe.transpose(bank[:, BANK_T + t % 2, b * P:(b + 1) * P],
                                                        stage[:, t, b * P:(b + 1) * P], ident[:, :])
                                last.then_inc(rot_tr.sem, 1)
                        n += 1
                with pe.Fori(0, 2) as kv:
                    with pe.Fori(0, 2) as r:
                        pair(l, kv * 2 + r, kv * (2 * T) + r * T, 0, True, kv * HD)
                with pe.Fori(0, 4) as h:
                    pair(l, h + 4, h * T + 4 * T, h * T, False, h * P + P)
                pe.wait_ge(mixT_lo_done.sem, mixT_lo_done.at(l, 2 * PAIRS - 1))
                for c in range(2):
                    for kk in range(0, KT, 2):
                        pe.wait_ge(w_lo_done.sem, w_lo_done.at(l, n))
                        for t in range(T):
                            if c and kk == 0:
                                pe.wait_ge(x_added.sem, x_added.at(l, t))
                            i = rows_product(l, t, n, 2, kk, COLS, hT, kk == 0, kk == KT - 2)
                            if kk == KT - 2:
                                i.then_inc(out_done.sem, 1)
                            elif t == T - 1:
                                i.then_inc(w_used.sem, 1)
                        n += 1
                for t in range(T):
                    transpose_rows(l, 1, t)
                f0 = 0
                for q, F in enumerate(FF_GROUPS):
                    nb = FFN_BASE[q]
                    with pe.Fori(0, F // 2) as i:
                        for j in range(2):
                            e = i * 2 + (f0 + j)
                            if q:
                                pe.wait_ge(x_added.sem, x_added.at(l, (2 * q + 2) * T - 1))
                            else:
                                pe.wait_ge(hT_lo_done.sem, hT_lo_done.at(l, 4 * T - 1))
                            pe.wait_ge(act_ready.sem, act_ready.at(l, e - 2))
                            for u, done in enumerate((gate_done, up_done)):
                                m = nb + 2 * j + u
                                pe.wait_ge(w_lo_done.sem, w_lo_done.at(l, i * 4 + m))
                                a_hi, a_lo = chunk(m, KT)
                                for half in range(2):
                                    cols = slice(half * HALF_TOK, (half + 1) * HALF_TOK)
                                    for k in range(KT):
                                        last = mm3(bank[:, 4 * j + 2 * u + half, 0:HALF_TOK], a_hi[:, k, :], a_lo[:, k, :],
                                                   hT_hi[:, k, cols], hT_lo[:, k, cols], k == 0, k == KT - 1)
                                last.then_inc(done.sem, 1)
                    for c in range(2):
                        for kk in range(0, F, 2):
                            m = nb + 2 * F + c * F // 2 + kk // 2
                            pe.wait_ge(w_lo_done.sem, w_lo_done.at(l, m))
                            if c == 0:
                                pe.wait_ge(actT_lo_done.sem, actT_lo_done.at(l, f0 + kk + 1))
                            for t in range(T):
                                if kk == 0 and c == 0 and t in (0, 4):
                                    pe.wait_ge(act_ready.sem, act_ready.at(l, f0 + F - 2 + t // 4))
                                if kk == 0 and c:
                                    pe.wait_ge(x_added.sem, x_added.at(l, (2 * q + 2) * T + t))
                                last = rows_product(l, t, m, 2, kk, COLS, actT, kk == 0, kk == F - 2)
                                if kk == F - 2:
                                    last.then_inc(down_done.sem, 1)
                                elif t == T - 1:
                                    last.then_inc(w_used.sem, 1)
                    f0 += F


_INS = ["x_prompt", "x_sample", "w_in", "w_out", "gqa_q_norm", "gqa_k_norm", "diff_lambda_q1",
        "diff_lambda_k1", "diff_lambda_q2", "diff_lambda_k2", "diff_sub_norm", "gains", "w_gate_up", "w_down"]
_OUTS = [(1, T_PROMPT * P, D), (1, T_SAMPLE * P, D)]


def _shape_constants():
    import numpy as np
    import math
    f = np.float32

    def angles(pos, dim):
        inv = f(10000.0) ** (-np.arange(0, dim, 2, dtype=f) / f(dim))
        ang = pos.astype(f)[:, None] * inv[None, :].astype(f)
        return np.cos(ang).astype(f), np.sin(ang).astype(f)

    t = np.arange(T_SAMPLE * P)
    tc, ts = angles(t, HD)
    rc, rs = angles(t // 64, HD // 2)
    cc, cs = angles(t % 64, HD // 2)
    tables = np.stack([np.concatenate([tc, tc], 1), np.concatenate([-ts, ts], 1),
                       np.concatenate([rc, rc, cc, cc], 1), np.concatenate([-rs, rs, -cs, cs], 1)])
    rope = np.ascontiguousarray(tables.reshape(4, T_SAMPLE, P, HD).transpose(2, 0, 1, 3)).astype(f)
    init = [0.8 - 0.6 * math.exp(-0.3 * l) for l in range(L)]
    laminit = np.broadcast_to(np.array([init, [(1.0 - i) * math.sqrt(2.0) for i in init]], f), (P, 2, L)).copy()
    return {"ident": np.eye(P, dtype=f), "rope": rope, "laminit": laminit}


def kernel(**inputs):
    import numpy as _np
    import concourse.bacc as _bacc
    from concourse import mybir as _mybir
    from concourse.bass_utils import run_bass_kernel_spmd as _run

    per_layer = _np.stack([_np.asarray(inputs["attn_norm"]), _np.asarray(inputs["ffn_norm"])], axis=1)
    inputs["gains"] = _np.concatenate([per_layer.reshape(2 * L, D), _np.asarray(inputs["final_norm"])[None]], axis=0)
    nc = _bacc.Bacc("TRN2", target_bir_lowering=False, num_devices=1)
    arrays, args = {}, []
    for name, a in [(n, inputs[n]) for n in _INS] + list(_shape_constants().items()):
        a = _np.ascontiguousarray(a)
        arrays[f"in_{name}_dram"] = a
        args.append(nc.dram_tensor(f"in_{name}_dram", a.shape, _mybir.dt.from_np(a.dtype), kind="ExternalInput").ap())
    for i, shape in enumerate(_OUTS):
        args.append(nc.dram_tensor(f"out_{i}_dram", shape, _mybir.dt.float32, kind="ExternalOutput").ap())
    build(nc, *args)
    r = _run(nc, [arrays], core_ids=[0])
    return tuple(r.results[0][f"out_{i}_dram"] for i in range(len(_OUTS)))
```

```python
import concourse.bass as bass
from concourse import mybir
from contextlib import ExitStack

F32 = mybir.dt.float32
F32R = mybir.dt.float32r
BF16 = mybir.dt.bfloat16
F16 = mybir.dt.float16
ALU = mybir.AluOpType
ACT = mybir.ActivationFunctionType
AX = mybir.AxisListType

P = 128
D = 1024
KT = D // P
T_PROMPT, T_SAMPLE = 2, 4
T = T_PROMPT + T_SAMPLE
TOK = T * P
HALF_TOK = TOK // 2
L = 2
HD = 64
GQA_Q, GQA_KV, DIFF_QK, DIFF_V = 512, 128, 512, 512
FF = 2816
FT = FF // P
EPS, SUB_EPS = 1e-6, 1e-5
PAIRS = 8
COLS = 512

PROJ = [(0, 512, 2, 8), (512, 256, 4, 2), (768, 512, 2, 8), (1280, 512, 2, 8), (1792, 512, 2, 0)]
FIRST_BLOCK = [0, 8, 4, 10]
N_BLOCKS = [4, 2, 4, 4]
FF_GROUPS = [8, 8, 6]

CHUNKS_IN = sum(KT // k for _, _, k, _ in PROJ)
CHUNKS_OUT = 2 * KT // 2
FFN_BASE = [CHUNKS_IN + CHUNKS_OUT + sum(3 * f for f in FF_GROUPS[:q]) for q in range(3)]
CHUNKS = CHUNKS_IN + CHUNKS_OUT + 3 * FT
RAW = 2
SPLIT = 2
assert CHUNKS % RAW == 0


P_SCALE = 2.0 ** 14


def seq_of(t):
    return (0, T_PROMPT * P, t) if t < T_PROMPT else (T_PROMPT * P, T_SAMPLE * P, t - T_PROMPT)


def build(nc, x_prompt, x_sample, w_in, w_out, gqa_q_norm, gqa_k_norm, lq1, lk1, lq2, lk2,
          diff_sub_norm, gains, w_gate_up, w_down, ident_c, rope_c, laminit_c, y_prompt, y_sample):
    ctx = ExitStack()
    with ctx:
        def sb(name, shape, dt=F32, where=ctx):
            return where.enter_context(nc.sbuf_tensor(name, shape, dt))

        class Signal:
            def __init__(self, name, per, credit=0):
                self.sem = ctx.enter_context(nc.semaphore(name))
                self.per, self.credit = per, credit

            def at(self, l, k):
                return l * self.per + (self.credit + 1 + k)

        x = sb("x", [P, T, D])
        hT_hi = sb("hT_hi", [P, KT, TOK], F32R)
        hT_lo = sb("hT_lo", [P, KT, TOK], F32R)
        w_raw = [sb(f"w_raw{s}", [P, 1024]) for s in range(RAW)]
        w_hi = [sb(f"w_hi{s}", [P, 1024], F32R) for s in range(SPLIT)]
        w_lo = [sb(f"w_lo{s}", [P, 1024], F32R) for s in range(SPLIT)]
        stage = sb("stage", [P, T, COLS])
        h_row = stage[:, :, :].rearrange("p (s a) c -> p s (a c)", a=2)
        prob = stage[:, 0:4, :].rearrange("p (b h) c -> p b h c", h=2)
        probT = stage[:, 4:6, :].bitcast(F16).rearrange("p h (s k q) -> p h s k q", s=2, q=P)
        gain = sb("gain", [P, D])
        ident = sb("ident", [P, P])
        rope = sb("rope", [P, 4, 4, HD])
        rope_g = sb("rope_g", [P, 4, 4, HD])
        qk_gain = sb("qk_gain", [P, 2, L, HD])
        lam_in = stage[:, 5, :].rearrange("p (i l d) -> p i l d", i=4, l=L)
        lam_prod = stage[:, 4, 0:2 * L * HD].rearrange("p (s l d) -> p s l d", s=2, l=L)
        lam_sum = sb("lam_sum", [P, 2, L])
        lam_exp = sb("lam_exp", [P, 2, L])
        lam_dif = sb("lam_dif", [P, L])
        lam_w = sb("lam_w", [P, 3, L])
        laminit = sb("laminit", [P, 2, L])
        map_w = sb("map_w", [P, 2])
        sub_all = sb("sub_all", [P, L, P])
        sub_gain = sb("sub_gain", [P, P])
        headsq = sb("headsq", [P, COLS])
        ss = sb("ss", [P, 1])
        ms = sb("ms", [P, 1])
        rstd = sb("rstd", [P, 1])
        hss = sb("hss", [P, 8])
        hms = sb("hms", [P, 8])
        hrstd = sb("hrstd", [P, 8])
        neg_half = sb("neg_half", [P, 8])
        eps_col = sb("eps_col", [P, 8])
        sub_eps = sb("sub_eps", [P, 1])
        neg_max = sb("neg_max", [P, 2, 2])
        row_sum = sb("row_sum", [P, 2, 2])
        inv_sum = sb("inv_sum", [P, 3, 2])
        row_w = sb("row_w", [P, 2])
        oss = sb("oss", [P, 1])
        oms = sb("oms", [P, 1])
        orstd = sb("orstd", [P, 1])
        xn = sb("xn", [P, COLS])

        with ExitStack() as attn:
            qkT = sb("qkT", [P, 14, TOK], F32, attn)
            v = [sb(f"v{i}", [P, T, 640], BF16, attn) for i in range(3)]
            q_hi = sb("q_hi", [P, TOK], F32R, attn)
            q_lo = sb("q_lo", [P, TOK], F32R, attn)
            k_hi = sb("k_hi", [P, TOK], F32R, attn)
            k_lo = sb("k_lo", [P, TOK], F32R, attn)
            mix = sb("mix", [P, T, P], F32, attn)
        with ExitStack() as ffn:
            actT_hi = sb("actT_hi", [P, max(FF_GROUPS), TOK], F32R, ffn)
            actT_lo = sb("actT_lo", [P, max(FF_GROUPS), TOK], F32R, ffn)
            silu = sb("silu", [P, 2, 2, HALF_TOK], F32, ffn)
        v_rest_gqa = headsq[:, COLS - P:COLS]
        rope_t = mix[:, 0:4, :].rearrange("p a b -> p (a b)")

        bank = ctx.enter_context(nc.psum_tensor("bank", [P, 8, 512], F32))
        BANK_T = 6
        BANK_PT, BANK_O, BANK_M = 4, 6, 7

        const_loaded = Signal("const_loaded", 0)
        x_loaded = Signal("x_loaded", 0)
        gain_loaded = Signal("gain_loaded", 2)
        w_loaded = [Signal(f"w_loaded{s}", CHUNKS // RAW) for s in range(RAW)]
        w_hi_done = Signal("w_hi_done", CHUNKS)
        w_lo_done = Signal("w_lo_done", CHUNKS, credit=RAW)
        w_used = Signal("w_used", CHUNKS - 2 * FT - 13, credit=1)
        setup = Signal("setup", 0)
        half_set = Signal("half_set", 0)
        lam_exp_done = Signal("lam_exp_done", 0)
        x_added = Signal("x_added", 48, credit=T)
        ss_done = Signal("ss_done", 2 * T)
        ms_done = Signal("ms_done", 2 * T)
        rstd_done = Signal("rstd_done", 2 * T)
        h_ready = Signal("h_ready", 2 * T)
        h_tr = Signal("h_tr", 4 * T)
        hT_hi_done = Signal("hT_hi_done", 4 * T)
        hT_lo_done = Signal("hT_lo_done", 4 * T)
        layer_consts = Signal("layer_consts", 1)
        proj_done = Signal("proj_done", 5 * T)
        headsq_done = Signal("headsq_done", 2 * T)
        hss_done = Signal("hss_done", 2 * T)
        hms_done = Signal("hms_done", 2 * T)
        hrstd_done = Signal("hrstd_done", 2 * T)
        xn_done = Signal("xn_done", 2 * T)
        rope_s_done = Signal("rope_s_done", 2 * T)
        rope_t_done = Signal("rope_t_done", 4 * T)
        rot_ready = Signal("rot_ready", 4 * T)
        rot_tr = Signal("rot_tr", 4 * T)
        qkT_done = Signal("qkT_done", 4 * T)
        v0_done = Signal("v0_done", 2 * T)
        v_rest = Signal("v_rest", 2 * T)
        v1_done = Signal("v1_done", 2 * T)
        v2_done = Signal("v2_done", 2 * T)
        qk_hi_done = Signal("qk_hi_done", 2 * PAIRS)
        qk_split = Signal("qk_split", 2 * PAIRS)
        scores_done = Signal("scores_done", PAIRS * T)
        max_done = Signal("max_done", PAIRS * T)
        exp_done = Signal("exp_done", PAIRS * T)
        inv_done = Signal("inv_done", PAIRS * T)
        row_w_done = Signal("row_w_done", 4 * T)
        p2_done = Signal("p2_done", 4 * T)
        p_comb = Signal("p_comb", 4 * T)
        pT_tr = [Signal("pT_tr0", PAIRS * T), Signal("pT_tr1", 4 * T)]
        pT_hi = [Signal("pT_hi0", PAIRS * T), Signal("pT_hi1", 4 * T)]
        pT_lo = [Signal("pT_lo0", PAIRS * T), Signal("pT_lo1", 4 * T)]
        o_done = Signal("o_done", PAIRS * T, credit=1)
        oss_done = Signal("oss_done", 4 * T)
        oms_done = Signal("oms_done", 4 * T)
        orstd_done = Signal("orstd_done", 4 * T)
        mix_ready = Signal("mix_ready", PAIRS * T, credit=3)
        mix_tr = Signal("mix_tr", 2 * PAIRS)
        mixT_hi_done = Signal("mixT_hi_done", 2 * PAIRS)
        mixT_lo_done = Signal("mixT_lo_done", 2 * PAIRS, credit=1)
        out_done = Signal("out_done", 2 * T)
        gate_done = Signal("gate_done", FT)
        up_done = Signal("up_done", FT)
        silu_done = Signal("silu_done", FT)
        act_ready = Signal("act_ready", FT, credit=2)
        actT_hi_done = Signal("actT_hi_done", FT)
        actT_lo_done = Signal("actT_lo_done", FT, credit=2)
        down_done = Signal("down_done", 6 * T, credit=1)
        y_ready = Signal("y_ready", 0)
        y_stored = [Signal(f"y_stored{s}", 0) for s in range(3)]

        USED = {-2: (w_used, -1), -1: (down_done, -1)}
        for g, (_, _, k, _) in enumerate(PROJ):
            for kk in range(0, KT, k):
                USED[len(USED) - 2] = (proj_done, g * T + T - 1) if kk == KT - k else (w_used, None)
        for c in range(2):
            for kk in range(0, KT, 2):
                USED[len(USED) - 2] = (out_done, c * T + T - 1) if kk == KT - 2 else (w_used, None)
        f0 = 0
        for q, F in enumerate(FF_GROUPS):
            for f in range(f0, f0 + F):
                USED[len(USED) - 2] = (gate_done, f)
                USED[len(USED) - 2] = (up_done, f)
            for c in range(2):
                for kk in range(0, F, 2):
                    USED[len(USED) - 2] = (down_done, (2 * q + c) * T + T - 1) if kk == F - 2 else (w_used, None)
            f0 += F
        count = 0
        for n in range(CHUNKS):
            if USED[n][1] is None:
                USED[n] = (w_used, count)
                count += 1
        assert count == w_used.per

        block = ctx.enter_context(nc.Block())

        def spread(ap, axis, n):
            shape = list(ap.shape)
            return ap.unsqueeze(axis).broadcast_to(shape[:axis] + [n] + shape[axis:])

        def one(ap):
            return ap.rearrange("p o c -> p (o c)")

        def at(i, n=1):
            return bass.ds(i, n)

        PARTS = (slice(0, T_PROMPT * P), slice(T_PROMPT * P, TOK))

        win = w_in.rearrange("l (k p) c -> l p k c", p=P)
        wout = w_out.rearrange("l (k p) c -> l p k c", p=P)
        wgu = w_gate_up.rearrange("l (k p) c -> l p k c", p=P)
        wdn = w_down.rearrange("l (k p) c -> l p k c", p=P)

        @block.sync
        def _(sp):
            for t in range(T):
                src = x_prompt[0, t * P:(t + 1) * P, :] if t < T_PROMPT else \
                    x_sample[0, (t - T_PROMPT) * P:(t - T_PROMPT + 1) * P, :]
                sp.dma_start(x[:, t, :], src).then_inc(x_loaded.sem, 16)

            def load(l, n, slot, src, k, cols):
                sp.wait_ge(w_lo_done.sem, w_lo_done.at(l, n - RAW))
                sp.dma_start(w_raw[slot][:, :].rearrange("p (k c) -> p k c", k=k),
                             src.rearrange("l p k c -> (l p) k c")).then_inc(w_loaded[slot].sem, 16)

            with sp.Fori(0, L) as l:
                n = 0
                for c0, cols, k, _ in PROJ:
                    for kk in range(0, KT, k):
                        load(l, n, n % RAW, win[at(l), :, kk:kk + k, c0:c0 + cols], k, cols)
                        n += 1
                for c in range(2):
                    for kk in range(0, KT, 2):
                        load(l, n, n % RAW, wout[at(l), :, kk:kk + 2, c * COLS:(c + 1) * COLS], 2, COLS)
                        n += 1
                f0 = 0
                for q, F in enumerate(FF_GROUPS):
                    nb = FFN_BASE[q]
                    with sp.Fori(0, F // 2) as i:
                        for j in range(2):
                            for u in range(2):
                                m = nb + 2 * j + u
                                load(l, m + i * 4, m % RAW,
                                     wgu[at(l), :, :, at(i * (2 * P) + ((f0 + j) * P + u * FF), P)], KT, P)
                    for c in range(2):
                        for kk in range(0, F, 2):
                            m = nb + 2 * F + c * F // 2 + kk // 2
                            load(l, m, m % RAW, wdn[at(l), :, f0 + kk:f0 + kk + 2, c * COLS:(c + 1) * COLS], 2, COLS)
                    f0 += F

            for t in range(T):
                dst = y_prompt[0, t * P:(t + 1) * P, :] if t < T_PROMPT else \
                    y_sample[0, (t - T_PROMPT) * P:(t - T_PROMPT + 1) * P, :]
                sp.wait_ge(y_ready.sem, t + 1)
                sp.dma_start(dst, h_row[:, t % 3, :]).then_inc(y_stored[t % 3].sem, 16)
            for s in range(3):
                sp.wait_ge(y_stored[s].sem, 16 * T // 3)

        @block.gpsimd
        def _(pool):
            def row(ap):
                return ap.partition_broadcast(P)

            pool.dma_start(gain[:, :], row(gains[0, :])).then_inc(gain_loaded.sem, 16)
            pool.dma_start(ident[:, :], ident_c).then_inc(const_loaded.sem, 16)
            pool.dma_start(rope[:, :, :, :], rope_c).then_inc(const_loaded.sem, 16)
            pool.dma_start(laminit[:, :, :], laminit_c).then_inc(const_loaded.sem, 16)
            for i, src in enumerate((gqa_q_norm, gqa_k_norm)):
                pool.dma_start(qk_gain[:, i, :, :].rearrange("p l d -> p (l d)"),
                               row(src.rearrange("l d -> (l d)"))).then_inc(const_loaded.sem, 16)
            for i, src in enumerate((lq1, lk1, lq2, lk2)):
                pool.dma_start(lam_in[:, i, :, :].rearrange("p l d -> p (l d)"),
                               row(src.rearrange("l d -> (l d)"))).then_inc(const_loaded.sem, 16)
            pool.dma_start(sub_all[:, :, :].rearrange("p l d -> p (l d)"),
                           row(diff_sub_norm.rearrange("l d -> (l d)"))).then_inc(const_loaded.sem, 16)
            pool.memset(neg_half[:, :], -0.5).then_inc(half_set.sem, 1)
            pool.memset(eps_col[:, :], EPS).then_inc(half_set.sem, 1)


            def inverse_rms(l, e, sums, sums_ready, mean, mean_ready, out, out_ready, eps, used, used_event):
                if used is not None:
                    pool.wait_ge(used.sem, used.at(l, used_event))
                pool.wait_ge(sums_ready.sem, sums_ready.at(l, e))
                pool.tensor_tensor(mean, sums, eps, ALU.add).then_inc(mean_ready.sem, 1)
                pool.wait_ge(mean_ready.sem, mean_ready.at(l, e))
                pool.tensor_tensor(out, mean, neg_half[:, 0:out.shape[1]], ALU.pow).then_inc(out_ready.sem, 1)

            def norm(l, m):
                for t in range(T):
                    e = m * T + t
                    inverse_rms(l, e, ss[:, :], ss_done, ms[:, :], ms_done, rstd[:, :], rstd_done, eps_col[:, 0:1],
                                h_ready if e else None, e - 1)

            pool.wait_ge(half_set.sem, 2)
            with pool.Fori(0, L) as l:
                norm(l, 0)
                pool.wait_ge(h_ready.sem, h_ready.at(l, T - 1))
                pool.dma_start(gain[:, :], row(gains[at(l * 2 + 1), :].rearrange("o c -> (o c)"))).then_inc(gain_loaded.sem, 16)
                for g in range(2):
                    heads = PROJ[g][3]
                    for t in range(T):
                        e = g * T + t
                        inverse_rms(l, e, hss[:, 0:heads], hss_done, hms[:, 0:heads], hms_done, hrstd[:, 0:heads],
                                    hrstd_done, eps_col[:, 0:heads], xn_done if e else None, e - 1)
                with pool.Fori(0, 4) as h:
                    for t in range(T):
                        inverse_rms(l, h * T + t, oss[:, :], oss_done, oms[:, :], oms_done, orstd[:, :], orstd_done,
                                    sub_eps[:, :], mix_ready, h * T + (4 * T + t - 1))
                norm(l, 1)
                pool.wait_ge(h_ready.sem, h_ready.at(l, 2 * T - 1))
                pool.dma_start(gain[:, :], row(gains[at(l * 2 + 2), :].rearrange("o c -> (o c)"))).then_inc(gain_loaded.sem, 16)
            for t in range(T):
                if t:
                    pool.wait_ge(y_ready.sem, t)
                inverse_rms(L, t, ss[:, :], ss_done, ms[:, :], ms_done, rstd[:, :], rstd_done, eps_col[:, 0:1], None, None)

        @block.scalar
        def _(act):
            def high(l, n0, turn, used, event):
                act.wait_ge(w_loaded[n0 % RAW].sem, (l * (CHUNKS // RAW) + (turn + 1)) * 16)
                act.wait_ge(used.sem, used.at(l, event))
                act.activation(w_hi[n0 % SPLIT][:, :], w_raw[n0 % RAW][:, :], ACT.Copy).then_inc(w_hi_done.sem, 1)

            def high_at(l, n):
                high(l, n, n // RAW, *USED[n - SPLIT])

            act.wait_ge(setup.sem, 2)
            act.activation(lam_exp[:, :, :], lam_sum[:, :, :], ACT.Exp).then_inc(lam_exp_done.sem, 1)

            def norm(l, m):
                for t in range(T + 1):
                    if t < T:
                        act.wait_ge(x_added.sem, x_added.at(l, (-T if m == 0 else T) + t))
                        act.wait_ge(ms_done.sem, ms_done.at(l, m * T + t - 1)) if m or t else None
                        act.activation(headsq[:, :].bitcast(BF16), x[:, t, :], ACT.Square,
                                       scale=D ** -0.5, accum_out=ss[:, :]).then_inc(ss_done.sem, 1)
                    if t:
                        for b in range(2):
                            e = 2 * (m * T + t - 1) + b
                            act.wait_ge(h_tr.sem, h_tr.at(l, e))
                            act.activation(hT_hi[:, 4 * b:4 * b + 4, (t - 1) * P:t * P],
                                           bank[:, BANK_T + b, :].rearrange("p (k q) -> p k q", q=P),
                                           ACT.Copy).then_inc(hT_hi_done.sem, 1)

            def copy_qkT(l, g, t):
                e = g * T + t
                act.wait_ge(rot_tr.sem, rot_tr.at(l, e))
                nb, b0 = N_BLOCKS[g], FIRST_BLOCK[g]
                act.activation(qkT[:, b0:b0 + nb, t * P:(t + 1) * P],
                               bank[:, BANK_T + t % 2, 0:nb * P].rearrange("p (k q) -> p k q", q=P),
                               ACT.Copy).then_inc(qkT_done.sem, 1)

            def read_projection(l, g, t, heads):
                e = g * T + t
                if g == 2 or g == 3:
                    return
                act.wait_ge(proj_done.sem, proj_done.at(l, e))
                if g == 1:
                    act.activation(v[0][:, t, 0:P], bank[:, t, P:2 * P], ACT.Copy).then_inc(v0_done.sem, 1)
                elif g == 4:
                    act.activation(v[0][:, t, P:P + DIFF_V], bank[:, t, :], ACT.Copy).then_inc(v0_done.sem, 1)
                if g < 2:
                    if e:
                        act.wait_ge(hss_done.sem, hss_done.at(l, e - 1))
                    act.activation(headsq[:, 0:heads * HD], bank[:, t, 0:heads * HD],
                                   ACT.Square, scale=HD ** -0.5).then_inc(headsq_done.sem, 1)
                if g in (1, 4):
                    e = t if g == 1 else T + t
                    act.wait_ge(v_rest.sem, v_rest.at(l, e))
                    out, rest = (v[1][:, t, 0:P], v_rest_gqa) if g == 1 else (v[1][:, t, P:P + DIFF_V], headsq[:, :])
                    act.activation(out, rest, ACT.Copy).then_inc(v1_done.sem, 1)

            def exps(l, e, t, last_use):
                S = seq_of(t)[1]
                b = t % 2
                act.wait_ge(max_done.sem, max_done.at(l, e))
                if last_use is not None:
                    act.wait_ge(last_use.sem, last_use.at(l, e - 2))
                act.activation(prob[:, b, 0, 0:S], bank[:, 2 * b, 0:S], ACT.Exp, bias=neg_max[:, b, 0:1],
                               accum_out=row_sum[:, b, 0:1])
                act.activation(prob[:, b, 1, 0:S], bank[:, 2 * b + 1, 0:S], ACT.Exp, bias=neg_max[:, b, 1:2],
                               accum_out=row_sum[:, b, 1:2]).then_inc(exp_done.sem, 1)

            def split_high(l, p, part, qb, kb):
                cols = PARTS[part]
                act.activation(q_hi[:, cols], one(qkT[:, at(qb), cols]), ACT.Copy, scale=HD ** -0.5)
                act.activation(k_hi[:, cols], one(qkT[:, at(kb), cols]), ACT.Copy).then_inc(qk_hi_done.sem, 1)

            def mixT_high(l, p, part):
                t0, n = (0, 2) if part == 0 else (2, 4)
                act.wait_ge(mix_tr.sem, mix_tr.at(l, p * 2 + part))
                act.activation(one(hT_hi[:, at(p), t0 * P:(t0 + n) * P]), bank[:, BANK_M, 0:n * P],
                               ACT.Copy).then_inc(mixT_hi_done.sem, 1)

            def probT_high(l, e, t, h, b):
                nk = seq_of(t)[1] // P
                act.wait_ge(pT_tr[h].sem, pT_tr[h].at(l, e))
                act.activation(probT[:, b, 0, 0:nk, :],
                               bank[:, BANK_PT + b, 0:nk * P].rearrange("p (k q) -> p k q", q=P), ACT.Copy,
                               scale=P_SCALE).then_inc(pT_hi[h].sem, 1)

            def pair(l, p, gqa, following):
                e0 = p * T
                last_use = pT_tr[1 if gqa else 0]
                for t in range(T + 1):
                    if not gqa and t < T:
                        for u in ((0, 1) if t == 0 else (t + 1,) if t + 1 < T else ()):
                            S = seq_of(u)[1]
                            act.wait_ge(row_w_done.sem, row_w_done.at(l, e0 + (u - 4 * T)))
                            act.activation(prob[:, u % 2, 1, 0:S], prob[:, u % 2, 1, 0:S], ACT.Copy,
                                           scale=row_w[:, 1:2]).then_inc(p2_done.sem, 1)
                    if not gqa and t:
                        act.wait_ge(o_done.sem, o_done.at(l, e0 + (t - 1)))
                        act.wait_ge(mix_ready.sem, mix_ready.at(l, e0 + (t - 2)))
                        act.activation(headsq[:, 0:P], bank[:, BANK_O, 0:P], ACT.Square, scale=1 / 8 / P_SCALE,
                                       accum_out=oss[:, :]).then_inc(oss_done.sem, 1)
                    if gqa and t < T:
                        act.wait_ge(o_done.sem, o_done.at(l, e0 + (t - 1)))
                        probT_high(l, e0 + t, t, 0, 0)
                        probT_high(l, e0 + t, t, 1, 1)
                    if t + 2 < T:
                        exps(l, e0 + (t + 2), t + 2, last_use)
                    elif t < T and following:
                        exps(l, e0 + (t + 2), t + 2 - T, last_use)
                    if not gqa and t < T:
                        act.wait_ge(o_done.sem, o_done.at(l, e0 + (t - 2)))
                        probT_high(l, e0 + t, t, 0, t % 2)
                    if following and t == 2:
                        split_high(l, p + 1, 0, *following)
                    if following and t == 4:
                        act.wait_ge(scores_done.sem, scores_done.at(l, e0 + (T - 1)))
                        split_high(l, p + 1, 1, *following)
                    if t == 3:
                        mixT_high(l, p, 0)
                mixT_high(l, p, 1)

            with act.Fori(0, L) as l:
                high_at(l, 0)
                high_at(l, 1)
                norm(l, 0)
                n = 0
                for g, (c0, cols, k, heads) in enumerate(PROJ):
                    for kk in range(0, KT, k):
                        if kk == 0 and g:
                            for t in range(T):
                                copy_qkT(l, g - 1, t)
                        last = kk == KT - k
                        for t in range(T):
                            if t == 3 and last:
                                high_at(l, n + 2)
                            if last:
                                read_projection(l, g, t, heads)
                        if not last:
                            high_at(l, n + 2)
                        n += 1
                act.wait_ge(qkT_done.sem, qkT_done.at(l, 4 * T - 1))
                split_high(l, 0, 0, 0, 8)
                split_high(l, 0, 1, 0, 8)
                exps(l, 0, 0, None)
                exps(l, 1, 1, None)
                with act.Fori(0, 2) as kv:
                    with act.Fori(0, 2) as r:
                        pair(l, kv * 2 + r, True, (kv * 2 + r + 1, kv + r + 8))
                with act.Fori(4, 7) as p:
                    pair(l, p, False, (p + 1, p + 7))
                pair(l, 7, False, None)
                for _ in range(CHUNKS_OUT):
                    high_at(l, n + 2)
                    n += 1
                norm(l, 1)
                f0 = 0
                for q, F in enumerate(FF_GROUPS):
                    nb = FFN_BASE[q]
                    with act.Fori(0, F // 2) as i:
                        for j in range(2):
                            e = i * 2 + (f0 + j)
                            act.wait_ge(gate_done.sem, gate_done.at(l, e))
                            act.wait_ge(actT_lo_done.sem, actT_lo_done.at(l, e - 2))
                            act.activation(silu[:, j, :, :], bank[:, 4 * j:4 * j + 2, 0:HALF_TOK],
                                           ACT.Silu).then_inc(silu_done.sem, 1)
                            m = nb + 2 * j + 2
                            high(l, m, i * (4 // RAW) + m // RAW, gate_done, e)
                            act.wait_ge(act_ready.sem, act_ready.at(l, e))
                            act.activation(one(actT_hi[:, at(i * 2 + j), :]),
                                           silu[:, j, :, :].rearrange("p a b -> p (a b)"),
                                           ACT.Copy).then_inc(actT_hi_done.sem, 1)
                            high(l, m + 1, i * (4 // RAW) + (m + 1) // RAW, up_done, e)
                    for m in range(nb + 2 * F, nb + 3 * F):
                        if m + 2 < CHUNKS:
                            high_at(l, m + 2)
                    f0 += F
            for t in range(T):
                act.wait_ge(x_added.sem, x_added.at(L, -T + t))
                act.wait_ge(ms_done.sem, ms_done.at(L, t - 1))
                act.activation(headsq[:, :].bitcast(BF16), x[:, t, :], ACT.Square,
                               scale=D ** -0.5, accum_out=ss[:, :]).then_inc(ss_done.sem, 1)

        @block.vector
        def _(dve):
            def low(l, n0, n):
                dve.wait_ge(w_hi_done.sem, w_hi_done.at(l, n))
                dve.tensor_tensor(w_lo[n0 % SPLIT][:, :], w_raw[n0 % RAW][:, :], w_hi[n0 % SPLIT][:, :].bitcast(F32),
                                  ALU.subtract).then_inc(w_lo_done.sem, 1)

            def norm(l, m):
                dve.wait_ge(gain_loaded.sem, (l * 2 + (m + 1)) * 16)
                for t in range(T + 1):
                    if t < T:
                        e = m * T + t
                        dve.wait_ge(rstd_done.sem, rstd_done.at(l, e))
                        if t >= 3:
                            dve.wait_ge(h_tr.sem, h_tr.at(l, 2 * (e - 3) + 1))
                        dve.scalar_tensor_tensor(h_row[:, t % 3, :], x[:, t, :], rstd[:, :], gain[:, :], ALU.mult,
                                                 ALU.mult).then_inc(h_ready.sem, 1)
                    if t:
                        for b in range(2):
                            e = 2 * (m * T + t - 1) + b
                            dve.wait_ge(hT_hi_done.sem, hT_hi_done.at(l, e))
                            dst = (slice(None), slice(4 * b, 4 * b + 4), slice((t - 1) * P, t * P))
                            dve.tensor_tensor(hT_lo[dst], bank[:, BANK_T + b, :].rearrange("p (k q) -> p k q", q=P),
                                              hT_hi[dst].bitcast(F32), ALU.subtract).then_inc(hT_lo_done.sem, 1)

            def value_parts(l, e, t, cols, src, rest):
                dve.wait_ge(v0_done.sem, v0_done.at(l, e))
                if e:
                    dve.wait_ge(v2_done.sem, v2_done.at(l, e - 1))
                dve.tensor_tensor(rest, src, v[0][:, t, cols], ALU.subtract).then_inc(v_rest.sem, 1)
                dve.wait_ge(v1_done.sem, v1_done.at(l, e))
                dve.tensor_tensor(v[2][:, t, cols], rest, v[1][:, t, cols], ALU.subtract).then_inc(v2_done.sem, 1)

            def rotate(l, g, t, heads):
                if g == 4:
                    value_parts(l, T + t, t, slice(P, P + DIFF_V), bank[:, t, :], headsq[:, :])
                    return
                e = g * T + t
                pos = seq_of(t)[2]
                W = heads * HD
                dve.wait_ge(proj_done.sem, proj_done.at(l, e))
                if g < 2:
                    dve.wait_ge(headsq_done.sem, headsq_done.at(l, e))
                    dve.tensor_reduce(hss[:, 0:heads], headsq[:, 0:W].rearrange("p (h d) -> p h d", d=HD), AX.X,
                                      ALU.add).then_inc(hss_done.sem, 1)
                    dve.wait_ge(hrstd_done.sem, hrstd_done.at(l, e))
                    if g == 1:
                        value_parts(l, t, t, slice(0, P), bank[:, t, P:2 * P], v_rest_gqa)
                    if e:
                        dve.wait_ge(rot_ready.sem, rot_ready.at(l, e - 1))
                    dve.tensor_tensor(xn[:, 0:W].rearrange("p (h d) -> p h d", d=HD),
                                      bank[:, t, 0:W].rearrange("p (h d) -> p h d", d=HD),
                                      spread(hrstd[:, 0:heads], 2, HD), ALU.mult).then_inc(xn_done.sem, 1)
                    dve.wait_ge(xn_done.sem, xn_done.at(l, e))
                    src = xn[:, 0:W]
                    cos, sin = rope_g[:, 2 * g, pos, :], rope_g[:, 2 * g + 1, pos, :]
                    groups, half = 2, HD // 4
                else:
                    src = bank[:, t, :]
                    cos, sin = rope[:, 0, pos, :], rope[:, 1, pos, :]
                    groups, half = 1, HD // 2
                if e and g >= 2:
                    dve.wait_ge(rot_ready.sem, rot_ready.at(l, e - 1))
                for a in range(2):
                    last = dve.tensor_tensor(
                        rope_t[:, 0:W].rearrange("p (h r a d) -> p h r a d", r=groups, a=2, d=half)[:, :, :, a, :],
                        src.rearrange("p (h r a d) -> p h r a d", r=groups, a=2, d=half)[:, :, :, 1 - a, :],
                        spread(sin.rearrange("p (r a d) -> p r a d", r=groups, a=2)[:, :, a, :], 1, heads), ALU.mult)
                if g < 2:
                    last.then_inc(rope_s_done.sem, 1)
                    dve.wait_ge(rope_s_done.sem, rope_s_done.at(l, e))
                dve.tensor_tensor(xn[:, 0:W].rearrange("p (h d) -> p h d", d=HD),
                                  src.rearrange("p (h d) -> p h d", d=HD), spread(cos, 1, heads),
                                  ALU.mult).then_inc(rope_t_done.sem, 1)
                dve.wait_ge(rope_t_done.sem, rope_t_done.at(l, e))
                if e >= T:
                    dve.wait_ge(rot_tr.sem, rot_tr.at(l, e - T))
                if g == 1:
                    dve.tensor_tensor(stage[:, t, 0:2 * W].rearrange("p (h r d) -> p h r d", r=2, d=HD),
                                      spread(xn[:, 0:W].rearrange("p (h d) -> p h d", d=HD), 2, 2),
                                      spread(rope_t[:, 0:W].rearrange("p (h d) -> p h d", d=HD), 2, 2),
                                      ALU.add).then_inc(rot_ready.sem, 1)
                else:
                    dve.tensor_tensor(stage[:, t, :], xn[:, :], rope_t[:, :], ALU.add).then_inc(rot_ready.sem, 1)

            def row_max(l, e, t):
                S = seq_of(t)[1]
                b = t % 2
                dve.wait_ge(scores_done.sem, scores_done.at(l, e))
                dve.tensor_reduce(neg_max[:, b, :], bank[:, 2 * b:2 * b + 2, 0:S], AX.X, ALU.max,
                                  negate=True).then_inc(max_done.sem, 1)

            def inverse_sums(l, e, t, gqa):
                dve.wait_ge(exp_done.sem, exp_done.at(l, e))
                dve.wait_ge(mix_ready.sem, mix_ready.at(l, e - 3))
                dve.reciprocal(inv_sum[:, t % 3, :], row_sum[:, t % 2, :]).then_inc(inv_done.sem, 1)
                if not gqa:
                    dve.wait_ge(inv_done.sem, inv_done.at(l, e))
                    dve.tensor_tensor(row_w[:, :], inv_sum[:, t % 3, :], map_w[:, :], ALU.mult).then_inc(row_w_done.sem, 1)

            def combine(l, e, t):
                S = seq_of(t)[1]
                b = t % 2
                dve.wait_ge(p2_done.sem, p2_done.at(l, e - 4 * T))
                dve.scalar_tensor_tensor(prob[:, b, 0, 0:S], prob[:, b, 0, 0:S], row_w[:, 0:1],
                                         prob[:, b, 1, 0:S], ALU.mult, ALU.add).then_inc(p_comb.sem, 1)

            def probT_low(l, e, t, h, b):
                nk = seq_of(t)[1] // P
                dve.wait_ge(pT_hi[h].sem, pT_hi[h].at(l, e))
                dve.scalar_tensor_tensor(probT[:, b, 1, 0:nk, :],
                                         bank[:, BANK_PT + b, 0:nk * P].rearrange("p (k q) -> p k q", q=P), P_SCALE,
                                         probT[:, b, 0, 0:nk, :], ALU.mult, ALU.subtract).then_inc(pT_lo[h].sem, 1)

            def split_low(l, p, part, qb, kb):
                cols = PARTS[part]
                dve.wait_ge(qk_hi_done.sem, qk_hi_done.at(l, p * 2 + part))
                dve.scalar_tensor_tensor(q_lo[:, cols], one(qkT[:, at(qb), cols]), HD ** -0.5,
                                         q_hi[:, cols].bitcast(F32), ALU.mult, ALU.subtract)
                dve.tensor_tensor(k_lo[:, cols], one(qkT[:, at(kb), cols]), k_hi[:, cols].bitcast(F32),
                                  ALU.subtract).then_inc(qk_split.sem, 1)

            def mixT_low(l, p, part):
                t0, n = (0, 2) if part == 0 else (2, 4)
                dve.wait_ge(mixT_hi_done.sem, mixT_hi_done.at(l, p * 2 + part))
                dve.tensor_tensor(one(hT_lo[:, at(p), t0 * P:(t0 + n) * P]), bank[:, BANK_M, 0:n * P],
                                  one(hT_hi[:, at(p), t0 * P:(t0 + n) * P]).bitcast(F32),
                                  ALU.subtract).then_inc(mixT_lo_done.sem, 1)

            def take_product(l, e, u, gqa):
                if gqa:
                    dve.wait_ge(o_done.sem, o_done.at(l, e))
                    dve.scalar_tensor_tensor(mix[:, u, :].rearrange("p (h d) -> p h d", d=HD),
                                             bank[:, BANK_O, 0:P].rearrange("p (h d) -> p h d", d=HD), 1 / P_SCALE,
                                             spread(inv_sum[:, u % 3, :], 2, HD), ALU.mult,
                                             ALU.mult).then_inc(mix_ready.sem, 1)
                else:
                    dve.wait_ge(orstd_done.sem, orstd_done.at(l, e - 4 * T))
                    dve.scalar_tensor_tensor(mix[:, u, :], bank[:, BANK_O, 0:P], orstd[:, :], sub_gain[:, :],
                                             ALU.mult, ALU.mult).then_inc(mix_ready.sem, 1)

            def pair(l, p, gqa, following):
                e0 = p * T
                for t in range(T + 1):
                    if t == 0:
                        inverse_sums(l, e0, 0, gqa)
                        if not gqa:
                            combine(l, e0, 0)
                    if t + 1 < T:
                        inverse_sums(l, e0 + (t + 1), t + 1, gqa)
                    if t + 2 < T:
                        row_max(l, e0 + (t + 2), t + 2)
                    elif t < T and following:
                        row_max(l, e0 + (t + 2), t + 2 - T)
                    if gqa:
                        if t:
                            take_product(l, e0 + (t - 1), t - 1, gqa)
                        if t < T:
                            probT_low(l, e0 + t, t, 0, 0)
                            probT_low(l, e0 + t, t, 1, 1)
                    else:
                        if t + 1 < T:
                            combine(l, e0 + (t + 1), t + 1)
                        if t < T:
                            probT_low(l, e0 + t, t, 0, t % 2)
                        if t:
                            take_product(l, e0 + (t - 1), t - 1, gqa)
                    if following and t == 2:
                        split_low(l, p + 1, 0, *following)
                    if following and t == 4:
                        split_low(l, p + 1, 1, *following)
                    if t == 3:
                        mixT_low(l, p, 0)
                mixT_low(l, p, 1)

            def add_to_x(l, e, done, ed, t, c):
                dve.wait_ge(done.sem, done.at(l, ed))
                xs = x[:, t, c * COLS:(c + 1) * COLS]
                dve.tensor_tensor(xs, xs, bank[:, t, :], ALU.add).then_inc(x_added.sem, 1)

            dve.sem_inc(w_lo_done.sem, RAW)
            dve.sem_inc(w_used.sem, 1)
            dve.sem_inc(down_done.sem, 1)
            dve.sem_inc(o_done.sem, 1)
            dve.sem_inc(mix_ready.sem, 3)
            dve.sem_inc(mixT_lo_done.sem, 1)
            dve.sem_inc(act_ready.sem, 2)
            dve.sem_inc(actT_lo_done.sem, 2)
            dve.wait_ge(x_loaded.sem, 16 * T)
            dve.sem_inc(x_added.sem, T)
            dve.wait_ge(const_loaded.sem, 16 * 10)
            pairs = lam_in[:, :, :, :].rearrange("p (s a) l d -> p s a (l d)", a=2)
            dve.tensor_tensor(lam_prod[:, :, :, :].rearrange("p s l d -> p s (l d)"), pairs[:, :, 0, :], pairs[:, :, 1, :],
                              ALU.mult).then_inc(setup.sem, 1)
            dve.wait_ge(setup.sem, 1)
            dve.tensor_reduce(lam_sum[:, :, :], lam_prod[:, :, :, :], AX.X, ALU.add).then_inc(setup.sem, 1)
            dve.wait_ge(lam_exp_done.sem, 1)
            dve.tensor_tensor(lam_dif[:, :], lam_exp[:, 1, :], lam_exp[:, 0, :], ALU.subtract).then_inc(setup.sem, 1)
            dve.wait_ge(setup.sem, 3)
            dve.tensor_tensor(lam_dif[:, :], lam_dif[:, :], laminit[:, 0, :], ALU.subtract).then_inc(setup.sem, 1)
            dve.wait_ge(setup.sem, 4)
            dve.tensor_scalar(lam_w[:, 0, :], lam_dif[:, :], -1.0, 1.0, ALU.mult, ALU.max).then_inc(setup.sem, 1)
            dve.wait_ge(setup.sem, 5)
            dve.tensor_tensor(lam_w[:, 0, :], lam_w[:, 0, :], lam_dif[:, :], ALU.max).then_inc(setup.sem, 1)
            dve.wait_ge(setup.sem, 6)
            dve.reciprocal(lam_w[:, 1, :], lam_w[:, 0, :]).then_inc(setup.sem, 1)
            dve.wait_ge(setup.sem, 7)
            dve.tensor_tensor(lam_w[:, 2, :], lam_w[:, 1, :], lam_dif[:, :], ALU.mult).then_inc(setup.sem, 1)
            dve.tensor_tensor(lam_w[:, 0, :], lam_w[:, 1, :], lam_w[:, 1, :], ALU.mult).then_inc(setup.sem, 1)
            dve.wait_ge(setup.sem, 9)

            with dve.Fori(0, L) as l:
                dve.tensor_copy(map_w[:, :], lam_w[:, 1:3, at(l)].rearrange("p s l -> p (s l)"))
                dve.tensor_scalar(sub_eps[:, :], lam_w[:, 0, at(l)], 2 * SUB_EPS, None, ALU.mult)
                dve.tensor_tensor(sub_gain[:, :], one(sub_all[:, at(l), :]), laminit[:, 1, at(l)].broadcast_to([P, P]),
                                  ALU.mult)
                for i in range(2):
                    g = one(qk_gain[:, i, at(l), :])
                    dve.tensor_tensor(rope_g[:, 2 * i, :, :], rope[:, 2, :, :], spread(g, 1, 4), ALU.mult)
                    for a in range(2):
                        def part(ap, which):
                            return ap.rearrange("p t (r a d) -> p t r a d", r=2, a=2)[:, :, :, which, :]
                        gs = g.rearrange("p (r a d) -> p r a d", r=2, a=2)[:, :, 1 - a, :]
                        last = dve.tensor_tensor(part(rope_g[:, 2 * i + 1, :, :], a), part(rope[:, 3, :, :], a),
                                                 spread(gs, 1, 4), ALU.mult)
                last.then_inc(layer_consts.sem, 1)
                dve.wait_ge(layer_consts.sem, layer_consts.at(l, 0))
                low(l, 0, 0)
                low(l, 1, 1)
                norm(l, 0)
                n = 0
                for g, (c0, cols, k, heads) in enumerate(PROJ):
                    for kk in range(0, KT, k):
                        last = kk == KT - k
                        for t in range(3 if last else 0):
                            rotate(l, g, t, heads)
                        low(l, n + 2, n + 2)
                        for t in range(3 if last else T, T):
                            rotate(l, g, t, heads)
                        n += 1
                split_low(l, 0, 0, 0, 8)
                split_low(l, 0, 1, 0, 8)
                row_max(l, 0, 0)
                row_max(l, 1, 1)
                with dve.Fori(0, 2) as kv:
                    with dve.Fori(0, 2) as r:
                        pair(l, kv * 2 + r, True, (kv * 2 + r + 1, kv + r + 8))
                with dve.Fori(4, 7) as p:
                    pair(l, p, False, (p + 1, p + 7))
                pair(l, 7, False, None)
                for c in range(2):
                    for kk in range(0, KT, 2):
                        if kk == KT - 2:
                            for t in range(T):
                                add_to_x(l, None, out_done, c * T + t, t, c)
                        low(l, n + 2, n + 2)
                        n += 1
                norm(l, 1)
                f0 = 0
                for q, F in enumerate(FF_GROUPS):
                    nb = FFN_BASE[q]
                    with dve.Fori(0, F // 2) as i:
                        for j in range(2):
                            e = i * 2 + (f0 + j)
                            m = nb + 2 * j + 2
                            low(l, m, m + i * 4)
                            dve.wait_ge(up_done.sem, up_done.at(l, e))
                            dve.wait_ge(silu_done.sem, silu_done.at(l, e))
                            s = silu[:, j, :, :]
                            dve.tensor_tensor(s, s, bank[:, 4 * j + 2:4 * j + 4, 0:HALF_TOK],
                                              ALU.mult).then_inc(act_ready.sem, 1)
                            dve.wait_ge(actT_hi_done.sem, actT_hi_done.at(l, e))
                            dst = at(i * 2 + j)
                            dve.tensor_tensor(one(actT_lo[:, dst, :]), silu[:, j, :, :].rearrange("p a b -> p (a b)"),
                                              one(actT_hi[:, dst, :]).bitcast(F32),
                                              ALU.subtract).then_inc(actT_lo_done.sem, 1)
                            low(l, m + 1, m + 1 + i * 4)
                    for c in range(2):
                        for kk in range(0, F, 2):
                            m = nb + 2 * F + c * F // 2 + kk // 2
                            if kk == F - 2:
                                for t in range(T):
                                    add_to_x(l, None, down_done, (2 * q + c) * T + t, t, c)
                            if m + 2 < CHUNKS:
                                low(l, m + 2, m + 2)
                    f0 += F
            dve.wait_ge(gain_loaded.sem, (2 * L + 1) * 16)
            for t in range(T):
                dve.wait_ge(rstd_done.sem, rstd_done.at(L, t))
                if t >= 3:
                    dve.wait_ge(y_stored[t % 3].sem, 16)
                dve.scalar_tensor_tensor(h_row[:, t % 3, :], x[:, t, :], rstd[:, :], gain[:, :], ALU.mult,
                                         ALU.mult).then_inc(y_ready.sem, 1)

        @block.tensor
        def _(pe):
            def mm3(out, a_hi, a_lo, b_hi, b_lo, first, last):
                pe.matmul(out, a_hi, b_hi, start=first, stop=False)
                pe.matmul(out, a_hi, b_lo, start=False, stop=False)
                return pe.matmul(out, a_lo, b_hi, start=False, stop=last)

            def chunk(n0, k):
                s = n0 % SPLIT
                return (w_hi[s][:, :].rearrange("p (k c) -> p k c", k=k),
                        w_lo[s][:, :].rearrange("p (k c) -> p k c", k=k))

            def transpose_rows(l, m, t):
                e = m * T + t
                pe.wait_ge(h_ready.sem, h_ready.at(l, e))
                for b in range(2):
                    if e:
                        pe.wait_ge(hT_lo_done.sem, hT_lo_done.at(l, 2 * e + b - 2))
                    for k in range(4):
                        last = pe.transpose(bank[:, BANK_T + b, k * P:(k + 1) * P],
                                            h_row[:, t % 3, (4 * b + k) * P:(4 * b + k + 1) * P], ident[:, :])
                    last.then_inc(h_tr.sem, 1)

            def rows_product(l, t, n0, k, kt0, cols, srcT, first, last):
                hi, lo = chunk(n0, k)
                a_hi, a_lo = srcT
                for kk in range(k):
                    i = mm3(bank[:, t, 0:cols], a_hi[:, kt0 + kk, t * P:(t + 1) * P], a_lo[:, kt0 + kk, t * P:(t + 1) * P],
                            hi[:, kk, :], lo[:, kk, :], first and kk == 0, last and kk == k - 1)
                return i

            def scores(l, e, t, split, banks_used):
                k0, S, _ = seq_of(t)
                b = t % 2
                if split is not None:
                    pe.wait_ge(qk_split.sem, qk_split.at(l, split))
                if banks_used:
                    pe.wait_ge(exp_done.sem, exp_done.at(l, e - 2))
                for h in range(2):
                    rows = slice(h * HD, (h + 1) * HD)
                    i = mm3(bank[:, 2 * b + h, 0:S], q_hi[rows, t * P:(t + 1) * P], q_lo[rows, t * P:(t + 1) * P],
                            k_hi[rows, k0:k0 + S], k_lo[rows, k0:k0 + S], True, True)
                i.then_inc(scores_done.sem, 1)

            def transpose_mix(l, p, part):
                t0, n = (0, 2) if part == 0 else (2, 4)
                pe.wait_ge(mix_ready.sem, mix_ready.at(l, p * T + (t0 + n - 1)))
                pe.wait_ge(mixT_lo_done.sem, mixT_lo_done.at(l, p * 2 + (part - 1)))
                for t in range(n):
                    last = pe.transpose(bank[:, BANK_M, t * P:(t + 1) * P], mix[:, t0 + t, :], ident[:, :])
                last.then_inc(mix_tr.sem, 1)

            def transpose_prob(l, e, t, gqa):
                b = t % 2
                nk = seq_of(t)[1] // P
                if gqa:
                    pe.wait_ge(exp_done.sem, exp_done.at(l, e))
                else:
                    pe.wait_ge(p_comb.sem, p_comb.at(l, e - 4 * T))
                    if t >= 2:
                        pe.wait_ge(pT_lo[0].sem, pT_lo[0].at(l, e - 2))
                for h in range(2 if gqa else 1):
                    if gqa and t:
                        pe.wait_ge(pT_lo[h].sem, pT_lo[h].at(l, e - 1))
                    for k in range(nk):
                        last = pe.transpose(bank[:, BANK_PT + (h if gqa else b), k * P:(k + 1) * P],
                                            prob[:, b, h, k * P:(k + 1) * P], ident[:, :])
                    last.then_inc(pT_tr[h].sem, 1)

            def product(l, e, t, gqa, vcol):
                k0, S, _ = seq_of(t)
                pe.wait_ge(mix_ready.sem, mix_ready.at(l, e - 1))
                for h in range(2 if gqa else 1):
                    pe.wait_ge(pT_lo[h].sem, pT_lo[h].at(l, e))
                    width = HD if gqa else P
                    out = bank[:, BANK_O, h * width:(h + 1) * width]
                    b = h if gqa else t % 2
                    terms = [(k, a, i) for k in range(S // P) for a, i in ((0, 0), (0, 1), (0, 2), (1, 0), (1, 1))]
                    for k, a, i in terms:
                        last = pe.matmul(out, probT[:, b, a, k, :], v[i][:, k0 // P + k, at(vcol, width)],
                                         start=(k, a, i) == terms[0], stop=(k, a, i) == terms[-1])
                last.then_inc(o_done.sem, 1)

            def pair(l, p, gqa, following, vcol):
                e0 = p * T
                for t in range(T):
                    if t + 2 < T:
                        scores(l, e0 + (t + 2), t + 2, p * 2 + 1 if t == 0 else None, True)
                    elif following and t == 4:
                        scores(l, e0 + T, 0, p * 2 + 2, True)
                    if t:
                        product(l, e0 + (t - 1), t - 1, gqa, vcol)
                    transpose_prob(l, e0 + t, t, gqa)
                    if t == 3:
                        transpose_mix(l, p, 0)
                if following:
                    scores(l, e0 + (T + 1), 1, None, True)
                product(l, e0 + (T - 1), T - 1, gqa, vcol)
                transpose_mix(l, p, 1)

            hT = (hT_hi, hT_lo)
            actT = (actT_hi, actT_lo)
            pe.wait_ge(const_loaded.sem, 16 * 10)
            with pe.Fori(0, L) as l:
                n = 0
                transpose_rows(l, 0, 0)
                for g, (c0, cols, k, heads) in enumerate(PROJ):
                    for kk in range(0, KT, k):
                        pe.wait_ge(w_lo_done.sem, w_lo_done.at(l, n))
                        for t in range(T):
                            if n == 0:
                                if t + 1 < T:
                                    transpose_rows(l, 0, t + 1)
                                pe.wait_ge(hT_lo_done.sem, hT_lo_done.at(l, 2 * t + 1))
                            if kk == 0 and g:
                                pe.wait_ge(rope_t_done.sem, rope_t_done.at(l, (g - 1) * T + t))
                            i = rows_product(l, t, n, k, kk, cols, hT, kk == 0, kk == KT - k)
                            if kk == KT - k:
                                i.then_inc(proj_done.sem, 1)
                            elif t == T - 1:
                                i.then_inc(w_used.sem, 1)
                            if kk == 0 and g:
                                e = (g - 1) * T + t
                                pe.wait_ge(rot_ready.sem, rot_ready.at(l, e))
                                if e >= 2:
                                    pe.wait_ge(qkT_done.sem, qkT_done.at(l, e - 2))
                                for b in range(N_BLOCKS[g - 1]):
                                    last = pe.transpose(bank[:, BANK_T + t % 2, b * P:(b + 1) * P],
                                                        stage[:, t, b * P:(b + 1) * P], ident[:, :])
                                last.then_inc(rot_tr.sem, 1)
                        n += 1
                pe.wait_ge(v2_done.sem, v2_done.at(l, 2 * T - 1))
                scores(l, 0, 0, 0, False)
                scores(l, 1, 1, None, False)
                with pe.Fori(0, 2) as kv:
                    with pe.Fori(0, 2) as r:
                        pair(l, kv * 2 + r, True, True, kv * HD)
                with pe.Fori(4, 7) as p:
                    pair(l, p, False, True, p * P - 3 * P)
                pair(l, 7, False, False, 4 * P)
                pe.wait_ge(mixT_lo_done.sem, mixT_lo_done.at(l, 2 * PAIRS - 1))
                for c in range(2):
                    for kk in range(0, KT, 2):
                        pe.wait_ge(w_lo_done.sem, w_lo_done.at(l, n))
                        for t in range(T):
                            if c and kk == 0:
                                pe.wait_ge(x_added.sem, x_added.at(l, t))
                            i = rows_product(l, t, n, 2, kk, COLS, hT, kk == 0, kk == KT - 2)
                            if kk == KT - 2:
                                i.then_inc(out_done.sem, 1)
                            elif t == T - 1:
                                i.then_inc(w_used.sem, 1)
                        n += 1
                for t in range(T):
                    transpose_rows(l, 1, t)
                f0 = 0
                for q, F in enumerate(FF_GROUPS):
                    nb = FFN_BASE[q]
                    with pe.Fori(0, F // 2) as i:
                        for j in range(2):
                            e = i * 2 + (f0 + j)
                            if q:
                                pe.wait_ge(x_added.sem, x_added.at(l, (2 * q + 2) * T - 1))
                            else:
                                pe.wait_ge(hT_lo_done.sem, hT_lo_done.at(l, 4 * T - 1))
                            pe.wait_ge(act_ready.sem, act_ready.at(l, e - 2))
                            for u, done in enumerate((gate_done, up_done)):
                                m = nb + 2 * j + u
                                pe.wait_ge(w_lo_done.sem, w_lo_done.at(l, i * 4 + m))
                                a_hi, a_lo = chunk(m, KT)
                                for half in range(2):
                                    cols = slice(half * HALF_TOK, (half + 1) * HALF_TOK)
                                    for k in range(KT):
                                        last = mm3(bank[:, 4 * j + 2 * u + half, 0:HALF_TOK], a_hi[:, k, :], a_lo[:, k, :],
                                                   hT_hi[:, k, cols], hT_lo[:, k, cols], k == 0, k == KT - 1)
                                last.then_inc(done.sem, 1)
                    for c in range(2):
                        for kk in range(0, F, 2):
                            m = nb + 2 * F + c * F // 2 + kk // 2
                            pe.wait_ge(w_lo_done.sem, w_lo_done.at(l, m))
                            if c == 0:
                                pe.wait_ge(actT_lo_done.sem, actT_lo_done.at(l, f0 + kk + 1))
                            for t in range(T):
                                if kk == 0 and c == 0 and t in (0, 4):
                                    pe.wait_ge(act_ready.sem, act_ready.at(l, f0 + F - 2 + t // 4))
                                if kk == 0 and c:
                                    pe.wait_ge(x_added.sem, x_added.at(l, (2 * q + 2) * T + t))
                                last = rows_product(l, t, m, 2, kk, COLS, actT, kk == 0, kk == F - 2)
                                if kk == F - 2:
                                    last.then_inc(down_done.sem, 1)
                                elif t == T - 1:
                                    last.then_inc(w_used.sem, 1)
                    f0 += F


_INS = ["x_prompt", "x_sample", "w_in", "w_out", "gqa_q_norm", "gqa_k_norm", "diff_lambda_q1",
        "diff_lambda_k1", "diff_lambda_q2", "diff_lambda_k2", "diff_sub_norm", "gains", "w_gate_up", "w_down"]
_OUTS = [(1, T_PROMPT * P, D), (1, T_SAMPLE * P, D)]


def _shape_constants():
    import numpy as np
    import math
    f = np.float32

    def angles(pos, dim):
        inv = f(10000.0) ** (-np.arange(0, dim, 2, dtype=f) / f(dim))
        ang = pos.astype(f)[:, None] * inv[None, :].astype(f)
        return np.cos(ang).astype(f), np.sin(ang).astype(f)

    t = np.arange(T_SAMPLE * P)
    tc, ts = angles(t, HD)
    rc, rs = angles(t // 64, HD // 2)
    cc, cs = angles(t % 64, HD // 2)
    tables = np.stack([np.concatenate([tc, tc], 1), np.concatenate([-ts, ts], 1),
                       np.concatenate([rc, rc, cc, cc], 1), np.concatenate([-rs, rs, -cs, cs], 1)])
    rope = np.ascontiguousarray(tables.reshape(4, T_SAMPLE, P, HD).transpose(2, 0, 1, 3)).astype(f)
    init = [0.8 - 0.6 * math.exp(-0.3 * l) for l in range(L)]
    laminit = np.broadcast_to(np.array([init, [(1.0 - i) * math.sqrt(2.0) / P_SCALE for i in init]], f), (P, 2, L)).copy()
    return {"ident": np.eye(P, dtype=f), "rope": rope, "laminit": laminit}


def kernel(**inputs):
    import numpy as _np
    import concourse.bacc as _bacc
    from concourse import mybir as _mybir
    from concourse.bass_utils import run_bass_kernel_spmd as _run

    per_layer = _np.stack([_np.asarray(inputs["attn_norm"]), _np.asarray(inputs["ffn_norm"])], axis=1)
    inputs["gains"] = _np.concatenate([per_layer.reshape(2 * L, D), _np.asarray(inputs["final_norm"])[None]], axis=0)
    nc = _bacc.Bacc("TRN2", target_bir_lowering=False, num_devices=1)
    arrays, args = {}, []
    for name, a in [(n, inputs[n]) for n in _INS] + list(_shape_constants().items()):
        a = _np.ascontiguousarray(a)
        arrays[f"in_{name}_dram"] = a
        args.append(nc.dram_tensor(f"in_{name}_dram", a.shape, _mybir.dt.from_np(a.dtype), kind="ExternalInput").ap())
    for i, shape in enumerate(_OUTS):
        args.append(nc.dram_tensor(f"out_{i}_dram", shape, _mybir.dt.float32, kind="ExternalOutput").ap())
    build(nc, *args)
    r = _run(nc, [arrays], core_ids=[0])
    return tuple(r.results[0][f"out_{i}_dram"] for i in range(len(_OUTS)))
```

```python
import concourse.bass as bass
from concourse import mybir
from contextlib import ExitStack

F32 = mybir.dt.float32
F32R = mybir.dt.float32r
BF16 = mybir.dt.bfloat16
F16 = mybir.dt.float16
ALU = mybir.AluOpType
ACT = mybir.ActivationFunctionType
AX = mybir.AxisListType

P = 128
D = 1024
KT = D // P
T_PROMPT, T_SAMPLE = 2, 4
T = T_PROMPT + T_SAMPLE
TOK = T * P
HALF_TOK = TOK // 2
L = 2
HD = 64
GQA_Q, GQA_KV, DIFF_QK, DIFF_V = 512, 128, 512, 512
FF = 2816
FT = FF // P
EPS, SUB_EPS = 1e-6, 1e-5
PAIRS = 8
COLS = 512

PROJ = [(512, 256, 4, 2), (0, 512, 2, 8), (768, 512, 2, 8), (1280, 512, 2, 8), (1792, 512, 2, 0)]
G_KV, G_Q, G_DQ, G_DK, G_DV = range(5)
FIRST_BLOCK = [8, 0, 4, 10]
N_BLOCKS = [2, 4, 4, 4]
FF_GROUPS = [8, 8, 6]

CHUNKS_IN = sum(KT // k for _, _, k, _ in PROJ)
CHUNKS_OUT = 2 * KT // 2
FFN_BASE = [CHUNKS_IN + CHUNKS_OUT + sum(3 * f for f in FF_GROUPS[:q]) for q in range(3)]
CHUNKS = CHUNKS_IN + CHUNKS_OUT + 3 * FT
RAW = 2
SPLIT = 2
assert CHUNKS % RAW == 0


P_SCALE = 2.0 ** 14
MAP_SCALE = 2.0 ** 5


def seq_of(t):
    return (0, T_PROMPT * P, t) if t < T_PROMPT else (T_PROMPT * P, T_SAMPLE * P, t - T_PROMPT)


def build(nc, x_prompt, x_sample, w_in, w_out, gqa_q_norm, gqa_k_norm, lam_vectors, sub_gains, gains, w_gate_up, w_down, ident_c, rope_c, laminit_c, y_prompt, y_sample):
    ctx = ExitStack()
    with ctx:
        def sb(name, shape, dt=F32, where=ctx):
            return where.enter_context(nc.sbuf_tensor(name, shape, dt))

        class Signal:
            def __init__(self, name, per, credit=0):
                self.sem = ctx.enter_context(nc.semaphore(name))
                self.per, self.credit = per, credit

            def at(self, l, k):
                return l * self.per + (self.credit + 1 + k)

        x = sb("x", [P, T, D])
        hT_hi = sb("hT_hi", [P, KT, TOK], F32R)
        hT_lo = sb("hT_lo", [P, KT, TOK], F32R)
        w_raw = [sb(f"w_raw{s}", [P, 1024]) for s in range(RAW)]
        w_hi = [sb(f"w_hi{s}", [P, 1024], F32R) for s in range(SPLIT)]
        w_lo = [sb(f"w_lo{s}", [P, 1024], F32R) for s in range(SPLIT)]
        stage = sb("stage", [P, T, COLS])
        h_row = stage[:, :, :].rearrange("p (s a) c -> p s (a c)", a=2)
        prob = stage[:, 0:4, :].rearrange("p (b h) c -> p b h c", h=2)
        probT = stage[:, 4:6, :].bitcast(F16).rearrange("p h (s k q) -> p h s k q", s=2, q=P)
        gain = sb("gain", [P, D])
        ident = sb("ident", [P, P])
        rope = sb("rope", [P, 4, 4, HD])
        rope_g = sb("rope_g", [P, 4, 4, HD])
        qk_gain = sb("qk_gain", [P, 2, L, HD])
        lam_in = stage[:, 5, :].rearrange("p (i l d) -> p i l d", i=4, l=L)
        lam_prod = stage[:, 4, 0:2 * L * HD].rearrange("p (s l d) -> p s l d", s=2, l=L)
        lam_sum = sb("lam_sum", [P, 2, L])
        lam_exp = sb("lam_exp", [P, 2, L])
        lam_dif = sb("lam_dif", [P, L])
        lam_s = sb("lam_s", [P, 2, L])
        laminit = sb("laminit", [P, 2, L])
        neg_lam = sb("neg_lam", [P, 1])
        map_scale = sb("map_scale", [P, 1])
        eps_root = sb("eps_root", [P, 1])
        sub_all = sb("sub_all", [P, L])
        sub_gain = sb("sub_gain", [P, 1])
        headsq = sb("headsq", [P, COLS])
        ss = sb("ss", [P, T])
        ms = sb("ms", [P, T])
        rstd = sb("rstd", [P, T])
        hss = sb("hss", [P, 2, 8])
        hms = sb("hms", [P, 2, 8])
        hrstd = sb("hrstd", [P, 2, 8])
        neg_half = sb("neg_half", [P, 8])
        eps_col = sb("eps_col", [P, 8])
        neg_max = sb("neg_max", [P, 2, 2])
        row_sum = sb("row_sum", [P, T, 2])
        inv_sum = sb("inv_sum", [P, T, 2])
        ratio = sb("ratio", [P, T])
        eps_row = sb("eps_row", [P, T])
        oss = sb("oss", [P, T])
        oms = sb("oms", [P, T])
        orstd = sb("orstd", [P, T])
        xn = sb("xn", [P, COLS])

        with ExitStack() as attn:
            qkT = sb("qkT", [P, 14, TOK], F32, attn)
            v = [sb(f"v{i}", [P, T, 640], BF16, attn) for i in range(3)]
            q_hi = sb("q_hi", [P, TOK], F32R, attn)
            q_lo = sb("q_lo", [P, TOK], F32R, attn)
            k_hi = sb("k_hi", [P, TOK], F32R, attn)
            k_lo = sb("k_lo", [P, TOK], F32R, attn)
            mix = sb("mix", [P, T, P], F32, attn)
        with ExitStack() as ffn:
            actT_hi = sb("actT_hi", [P, max(FF_GROUPS), TOK], F32R, ffn)
            actT_lo = sb("actT_lo", [P, max(FF_GROUPS), TOK], F32R, ffn)
            silu = sb("silu", [P, 2, 2, HALF_TOK], F32, ffn)
        v_rest_kv = [headsq[:, P:2 * P], headsq[:, 2 * P:3 * P]]
        v_rest_dv = [headsq[:, :], xn[:, :]]
        junk = [headsq[:, :].bitcast(BF16), xn[:, :].bitcast(BF16)]
        rope_t = mix[:, 0:4, :].rearrange("p a b -> p (a b)")

        bank = ctx.enter_context(nc.psum_tensor("bank", [P, 8, 512], F32))
        BANK_T = 6
        BANK_PT, BANK_O = 4, 6
        BANK_M = 7

        const_loaded = Signal("const_loaded", 0)
        lam_loaded = Signal("lam_loaded", 0)
        laminit_loaded = Signal("laminit_loaded", 0)
        ident_loaded = Signal("ident_loaded", 0)
        x_loaded = [Signal(f"x_loaded{t}", 0) for t in range(T)]
        gain_loaded = Signal("gain_loaded", 2)
        w_loaded = [Signal(f"w_loaded{s}", CHUNKS // RAW) for s in range(RAW)]
        w_hi_done = Signal("w_hi_done", CHUNKS)
        w_lo_done = Signal("w_lo_done", CHUNKS, credit=RAW)
        w_used = Signal("w_used", CHUNKS - 2 * FT - 13, credit=1)
        setup = Signal("setup", 0)
        half_set = Signal("half_set", 0)
        lam_exp_done = Signal("lam_exp_done", 0)
        x_added = Signal("x_added", 48, credit=T)
        ss_done = Signal("ss_done", 2 * T)
        ms_done = Signal("ms_done", 2 * T)
        rstd_done = Signal("rstd_done", 2 * T)
        h_ready = Signal("h_ready", 2 * T)
        h_tr = Signal("h_tr", 4 * T)
        hT_hi_done = Signal("hT_hi_done", 4 * T)
        hT_lo_done = Signal("hT_lo_done", 4 * T)
        layer_consts = Signal("layer_consts", 1)
        proj_done = Signal("proj_done", 5 * T)
        headsq_done = Signal("headsq_done", 2 * T)
        hss_done = Signal("hss_done", 2 * T)
        hms_done = Signal("hms_done", 2 * T)
        hrstd_done = Signal("hrstd_done", 2 * T)
        scaled = Signal("scaled", 2 * T)
        copied = Signal("copied", 2 * T)
        rope_t_done = Signal("rope_t_done", 4 * T)
        rot_ready = Signal("rot_ready", 4 * T)
        rot_tr = Signal("rot_tr", 4 * T)
        qkT_done = Signal("qkT_done", 4 * T)
        v0_done = Signal("v0_done", 2 * T)
        v_rest = Signal("v_rest", 2 * T)
        v1_done = Signal("v1_done", 2 * T)
        v2_done = Signal("v2_done", 2 * T)
        qk_hi_done = Signal("qk_hi_done", 4 * PAIRS)
        qk_split = Signal("qk_split", 4 * PAIRS)
        scores_done = Signal("scores_done", 2 * PAIRS * T)
        max_done = Signal("max_done", 2 * PAIRS * T)
        exp_done = Signal("exp_done", 2 * PAIRS * T)
        inv_done = Signal("inv_done", PAIRS * T)
        ratio_done = Signal("ratio_done", 4 * T)
        p_comb = Signal("p_comb", 4 * T)
        pT_tr = [Signal("pT_tr0", PAIRS * T), Signal("pT_tr1", 4 * T)]
        pT_hi = [Signal("pT_hi0", PAIRS * T), Signal("pT_hi1", 4 * T)]
        pT_lo = [Signal("pT_lo0", PAIRS * T), Signal("pT_lo1", 4 * T)]
        o_done = Signal("o_done", PAIRS * T)
        oss_done = Signal("oss_done", 4 * T)
        oms_done = Signal("oms_done", 4 * T)
        orstd_done = Signal("orstd_done", 4 * T)
        mix_gqa = Signal("mix_gqa", 4 * T, credit=2)
        mix_diff = Signal("mix_diff", 4 * T, credit=2)
        mix_tr = Signal("mix_tr", 2 * PAIRS)
        mixT_hi_done = Signal("mixT_hi_done", 2 * PAIRS)
        mixT_lo_done = Signal("mixT_lo_done", 2 * PAIRS, credit=1)
        out_done = Signal("out_done", 2 * T)
        gate_done = Signal("gate_done", FT)
        up_done = Signal("up_done", FT)
        silu_done = Signal("silu_done", FT)
        act_ready = Signal("act_ready", FT, credit=2)
        actT_hi_done = Signal("actT_hi_done", FT)
        actT_lo_done = Signal("actT_lo_done", FT, credit=2)
        down_done = Signal("down_done", 6 * T, credit=1)
        y_stored = [Signal(f"y_stored{s}", 0) for s in range(3)]

        USED = {-2: (w_used, -1), -1: (down_done, -1)}
        for g, (_, _, k, _) in enumerate(PROJ):
            for kk in range(0, KT, k):
                USED[len(USED) - 2] = (proj_done, g * T + T - 1) if kk == KT - k else (w_used, None)
        for c in range(2):
            for kk in range(0, KT, 2):
                USED[len(USED) - 2] = (out_done, c * T + T - 1) if kk == KT - 2 else (w_used, None)
        f0 = 0
        for q, F in enumerate(FF_GROUPS):
            for f in range(f0, f0 + F):
                USED[len(USED) - 2] = (gate_done, f)
                USED[len(USED) - 2] = (up_done, f)
            for c in range(2):
                for kk in range(0, F, 2):
                    USED[len(USED) - 2] = (down_done, (2 * q + c) * T + T - 1) if kk == F - 2 else (w_used, None)
            f0 += F
        count = 0
        for n in range(CHUNKS):
            if USED[n][1] is None:
                USED[n] = (w_used, count)
                count += 1
        assert count == w_used.per

        block = ctx.enter_context(nc.Block())

        def spread(ap, axis, n):
            shape = list(ap.shape)
            return ap.unsqueeze(axis).broadcast_to(shape[:axis] + [n] + shape[axis:])

        def one(ap):
            return ap.rearrange("p o c -> p (o c)")

        def at(i, n=1):
            return bass.ds(i, n)

        PARTS = (slice(0, T_PROMPT * P), slice(T_PROMPT * P, TOK))

        win = w_in.rearrange("l (k p) c -> l p k c", p=P)
        wout = w_out.rearrange("l (k p) c -> l p k c", p=P)
        wgu = w_gate_up.rearrange("l (k p) c -> l p k c", p=P)
        wdn = w_down.rearrange("l (k p) c -> l p k c", p=P)

        def load_x(engine, t):
            src = x_prompt[0, t * P:(t + 1) * P, :] if t < T_PROMPT else \
                x_sample[0, (t - T_PROMPT) * P:(t - T_PROMPT + 1) * P, :]
            engine.dma_start(x[:, t, :], src).then_inc(x_loaded[t].sem, 16)

        def row(ap):
            return ap.partition_broadcast(P)

        @block.sync
        def _(sp):
            load_x(sp, 0)
            sp.dma_start(ident[:, :], ident_c).then_inc(ident_loaded.sem, 16)
            sp.dma_start(laminit[:, :, :], laminit_c).then_inc(laminit_loaded.sem, 16)
            load_x(sp, 1)

            def load(l, last, slot, src, k, cols):
                if last is not None:
                    sp.wait_ge(w_lo_done.sem, w_lo_done.at(l, last))
                sp.dma_start(w_raw[slot][:, :].rearrange("p (k c) -> p k c", k=k),
                             src.rearrange("l p k c -> (l p) k c")).then_inc(w_loaded[slot].sem, 16)

            with sp.Fori(0, L) as l:
                n = 0
                for c0, cols, k, _ in PROJ:
                    for kk in range(0, KT, k):
                        load(l, {1: 0, 2: None}.get(n, n - RAW), n % RAW, win[at(l), :, kk:kk + k, c0:c0 + cols], k, cols)
                        n += 1
                for c in range(2):
                    for kk in range(0, KT, 2):
                        load(l, n - RAW, n % RAW, wout[at(l), :, kk:kk + 2, c * COLS:(c + 1) * COLS], 2, COLS)
                        n += 1
                f0 = 0
                for q, F in enumerate(FF_GROUPS):
                    nb = FFN_BASE[q]
                    with sp.Fori(0, F // 2) as i:
                        for j in range(2):
                            for u in range(2):
                                m = nb + 2 * j + u
                                load(l, i * 4 + (m - RAW), m % RAW,
                                     wgu[at(l), :, :, at(i * (2 * P) + ((f0 + j) * P + u * FF), P)], KT, P)
                    for c in range(2):
                        for kk in range(0, F, 2):
                            m = nb + 2 * F + c * F // 2 + kk // 2
                            load(l, m - RAW, m % RAW, wdn[at(l), :, f0 + kk:f0 + kk + 2, c * COLS:(c + 1) * COLS], 2, COLS)
                    f0 += F

            for t in range(T):
                dst = y_prompt[0, t * P:(t + 1) * P, :] if t < T_PROMPT else \
                    y_sample[0, (t - T_PROMPT) * P:(t - T_PROMPT + 1) * P, :]
                sp.wait_ge(h_ready.sem, h_ready.at(L, t))
                sp.dma_start(dst, h_row[:, t % 3, :]).then_inc(y_stored[t % 3].sem, 16)
            for s in range(3):
                sp.wait_ge(y_stored[s].sem, 16 * T // 3)

        @block.gpsimd
        def _(pool):
            pool.dma_start(gain[:, :], row(gains[0, :])).then_inc(gain_loaded.sem, 16)
            for i, src in enumerate((gqa_q_norm, gqa_k_norm)):
                pool.dma_start(qk_gain[:, i, :, :].rearrange("p l d -> p (l d)"),
                               row(src.rearrange("l d -> (l d)"))).then_inc(const_loaded.sem, 16)
            pool.dma_start(sub_all[:, :], sub_gains).then_inc(const_loaded.sem, 16)
            pool.dma_start(rope[:, :, :, :], rope_c).then_inc(const_loaded.sem, 16)
            pool.memset(neg_half[:, :], -0.5).then_inc(half_set.sem, 1)
            pool.memset(eps_col[:, :], EPS).then_inc(half_set.sem, 1)


            def inverse_rms(l, e, sums, sums_ready, mean, mean_ready, out, out_ready, eps, used, used_event):
                if used is not None:
                    pool.wait_ge(used.sem, used.at(l, used_event))
                pool.wait_ge(sums_ready.sem, sums_ready.at(l, e))
                pool.tensor_tensor(mean, sums, eps, ALU.add).then_inc(mean_ready.sem, 1)
                pool.wait_ge(mean_ready.sem, mean_ready.at(l, e))
                pool.tensor_tensor(out, mean, neg_half[:, 0:out.shape[1]], ALU.pow).then_inc(out_ready.sem, 1)

            def norm(l, m):
                for t in range(T):
                    e = m * T + t
                    c = slice(t, t + 1)
                    inverse_rms(l, e, ss[:, c], ss_done, ms[:, c], ms_done, rstd[:, c], rstd_done, eps_col[:, 0:1],
                                None, None)

            def split_low(l, p, part, i, b):
                cols = PARTS[part]
                hi, lo = ((q_hi, q_lo), (k_hi, k_lo))[i]
                pool.wait_ge(qk_hi_done.sem, qk_hi_done.at(l, p * 4 + (2 * part + i)))
                pool.tensor_tensor(lo[:, cols], one(qkT[:, at(b), cols]), hi[:, cols].bitcast(F32),
                                   ALU.subtract).then_inc(qk_split.sem, 1)

            def head_rms(l, p, t):
                c = slice(t, t + 1)
                inverse_rms(l, (p - 4) * T + t, oss[:, c], oss_done, oms[:, c], oms_done, orstd[:, c], orstd_done,
                            eps_row[:, c], None, None)

            pool.wait_ge(half_set.sem, 2)
            with pool.Fori(0, L) as l:
                norm(l, 0)
                pool.wait_ge(h_ready.sem, h_ready.at(l, T - 1))
                pool.dma_start(gain[:, :], row(gains[at(l * 2 + 1), :].rearrange("o c -> (o c)"))).then_inc(gain_loaded.sem, 16)
                for g in range(2):
                    heads = PROJ[g][3]
                    for t in range(T):
                        e = g * T + t
                        b = t % 2
                        inverse_rms(l, e, hss[:, b, 0:heads], hss_done, hms[:, b, 0:heads], hms_done,
                                    hrstd[:, b, 0:heads], hrstd_done, eps_col[:, 0:heads],
                                    scaled if e >= 2 else None, e - 2)
                for part in range(2):
                    split_low(l, 0, part, 0, 0)
                    split_low(l, 0, part, 1, 8)
                with pool.Fori(0, 2) as kv:
                    with pool.Fori(0, 2) as r:
                        for part in range(2):
                            split_low(l, kv * 2 + r + 1, part, 0, kv * 2 + r + 1)
                            split_low(l, kv * 2 + r + 1, part, 1, kv + r + 8)
                with pool.Fori(4, 7) as p:
                    for t in range(T):
                        head_rms(l, p, t)
                        if t in (0, 2):
                            split_low(l, p + 1, t // 2, 0, p + 1)
                            split_low(l, p + 1, t // 2, 1, p + 7)
                for t in range(T):
                    head_rms(l, 7, t)
                norm(l, 1)
                pool.wait_ge(h_ready.sem, h_ready.at(l, 2 * T - 1))
                pool.dma_start(gain[:, :], row(gains[at(l * 2 + 2), :].rearrange("o c -> (o c)"))).then_inc(gain_loaded.sem, 16)
            norm(L, 0)

        @block.scalar
        def _(act):
            def high(l, n0, turn, used, event):
                act.wait_ge(w_loaded[n0 % RAW].sem, (l * (CHUNKS // RAW) + (turn + 1)) * 16)
                act.wait_ge(used.sem, used.at(l, event))
                act.activation(w_hi[n0 % SPLIT][:, :], w_raw[n0 % RAW][:, :], ACT.Copy).then_inc(w_hi_done.sem, 1)

            def high_at(l, n):
                high(l, n, n // RAW, *USED[n - SPLIT])

            act.dma_start(lam_in[:, :, :, :].rearrange("p i l d -> p (i l d)"),
                          row(lam_vectors.rearrange("i l d -> (i l d)"))).then_inc(lam_loaded.sem, 16)
            for t in range(2, T):
                load_x(act, t)
            act.wait_ge(setup.sem, 2)
            act.activation(lam_exp[:, :, :], lam_sum[:, :, :], ACT.Exp).then_inc(lam_exp_done.sem, 1)

            def row_squares(l, m, t):
                act.wait_ge(x_added.sem, x_added.at(l, (-T if m == 0 else T) + t))
                act.wait_ge(x_loaded[t].sem, 16)
                if t >= 2:
                    act.wait_ge(ss_done.sem, ss_done.at(l, m * T + t - 2))
                act.activation(junk[t % 2], x[:, t, :], ACT.Square, scale=D ** -0.5,
                               accum_out=ss[:, t:t + 1]).then_inc(ss_done.sem, 1)

            def transposed_high(l, m, t):
                for b in range(2):
                    e = 2 * (m * T + t) + b
                    act.wait_ge(h_tr.sem, h_tr.at(l, e))
                    act.activation(hT_hi[:, 4 * b:4 * b + 4, t * P:(t + 1) * P],
                                   bank[:, BANK_T + b, :].rearrange("p (k q) -> p k q", q=P),
                                   ACT.Copy).then_inc(hT_hi_done.sem, 1)

            def early_squares(l, m):
                for t in range(3):
                    row_squares(l, m, t)

            def norm(l, m, chunk):
                for t in range(T):
                    transposed_high(l, m, t)
                    if t + 3 < T:
                        row_squares(l, m, t + 3)
                    if t == 1:
                        high_at(l, chunk)

            def copy_qkT(l, g, t):
                e = g * T + t
                act.wait_ge(rot_tr.sem, rot_tr.at(l, e))
                nb, b0 = N_BLOCKS[g], FIRST_BLOCK[g]
                act.activation(qkT[:, b0:b0 + nb, t * P:(t + 1) * P],
                               bank[:, BANK_T + t % 2, 0:nb * P].rearrange("p (k q) -> p k q", q=P), ACT.Copy,
                               scale=HD ** -0.5 if g in (G_Q, G_DQ) else 1.0).then_inc(qkT_done.sem, 1)

            def head_squares(l, g, t):
                e = g * T + t
                heads = PROJ[g][3]
                if e:
                    act.wait_ge(hss_done.sem, hss_done.at(l, e - 1))
                act.activation(headsq[:, 0:heads * HD], bank[:, t, 0:heads * HD],
                               ACT.Square, scale=HD ** -0.5).then_inc(headsq_done.sem, 1)

            def second_part(l, g, t):
                act.wait_ge(v_rest.sem, v_rest.at(l, t if g == G_KV else T + t))
                out, rest = (v[1][:, t, 0:P], v_rest_kv) if g == G_KV else (v[1][:, t, P:P + DIFF_V], v_rest_dv)
                act.activation(out, rest[t % 2], ACT.Copy).then_inc(v1_done.sem, 1)

            def read_projection(l, g):
                for t in range(T + 1):
                    if t < T:
                        act.wait_ge(proj_done.sem, proj_done.at(l, g * T + t))
                    if t < T and g == G_KV:
                        act.activation(v[0][:, t, 0:P], bank[:, t, P:2 * P], ACT.Copy).then_inc(v0_done.sem, 1)
                    if t < T and g == G_DV:
                        act.activation(v[0][:, t, P:P + DIFF_V], bank[:, t, :], ACT.Copy).then_inc(v0_done.sem, 1)
                    if t < T and g in (G_KV, G_Q):
                        head_squares(l, g, t)
                    if t < T and g in (G_DQ, G_DK):
                        act.activation(stage[:, t, :], bank[:, t, :], ACT.Copy).then_inc(copied.sem, 1)
                    if t and g in (G_KV, G_DV):
                        second_part(l, g, t - 1)

            def exp(l, e, t, h):
                S = seq_of(t)[1]
                b = t % 2
                act.wait_ge(max_done.sem, max_done.at(l, e * 2 + h))
                act.activation(prob[:, b, h, 0:S], bank[:, 2 * b + h, 0:S], ACT.Exp, bias=neg_max[:, b, h:h + 1],
                               accum_out=row_sum[:, t, h:h + 1]).then_inc(exp_done.sem, 1)

            def split_high(part, dst, b):
                cols = PARTS[part]
                act.activation(dst[:, cols], one(qkT[:, at(b), cols]), ACT.Copy).then_inc(qk_hi_done.sem, 1)

            def mixT_high(l, p, part, gqa):
                t0, n = (0, 2) if part == 0 else (2, 4)
                act.wait_ge(mix_tr.sem, mix_tr.at(l, p * 2 + part))
                act.activation(one(hT_hi[:, at(p), t0 * P:(t0 + n) * P]), bank[:, BANK_M, 0:n * P],
                               ACT.Copy, scale=1.0 if gqa else sub_gain[:, :]).then_inc(mixT_hi_done.sem, 1)

            def probT_high(l, e, t, h, b, scale):
                nk = seq_of(t)[1] // P
                act.wait_ge(pT_tr[h].sem, pT_tr[h].at(l, e))
                act.activation(probT[:, b, 0, 0:nk, :],
                               bank[:, BANK_PT + b, 0:nk * P].rearrange("p (k q) -> p k q", q=P), ACT.Copy,
                               scale=scale).then_inc(pT_hi[h].sem, 1)

            def gqa_pair(l, p, following):
                e0 = p * T
                for t in range(T):
                    probT_high(l, e0 + t, t, 0, 0, P_SCALE)
                    if t:
                        exp(l, e0 + (t + 1), (t + 1) % T, 1)
                    probT_high(l, e0 + t, t, 1, 1, P_SCALE)
                    exp(l, e0 + (t + 2), (t + 2) % T, 0)
                    if t == 2:
                        mixT_high(l, p, 0, True)
                    if t in (2, 4):
                        split_high(t // 2 - 1, q_hi, following[0])
                        split_high(t // 2 - 1, k_hi, following[1])
                exp(l, e0 + (T + 1), 1, 1)
                mixT_high(l, p, 1, True)

            def squares(l, p, t):
                act.wait_ge(o_done.sem, o_done.at(l, p * T + t))
                b = t % 2
                act.activation(headsq[:, b * P:(b + 1) * P], bank[:, BANK_O + b, 0:P], ACT.Square,
                               scale=1 / 8, accum_out=oss[:, t:t + 1]).then_inc(oss_done.sem, 1)

            def normed(l, p, t):
                act.wait_ge(orstd_done.sem, orstd_done.at(l, (p - 4) * T + t))
                act.activation(mix[:, t, :], bank[:, BANK_O + t % 2, 0:P], ACT.Copy,
                               scale=orstd[:, t:t + 1]).then_inc(mix_diff.sem, 1)

            def diff_pair(l, p, following):
                e0 = p * T
                for t in range(T):
                    if following and t == 4:
                        split_high(1, k_hi, following[1])
                    act.wait_ge(exp_done.sem, exp_done.at(l, (e0 + t) * 2))
                    act.activation(eps_row[:, t:t + 1], row_sum[:, t, 0:1], ACT.Square, scale=eps_root[:, :])
                    probT_high(l, e0 + t, t, 0, t % 2, map_scale[:, :])
                    if t >= 2:
                        normed(l, p, t - 2)
                    if t == T - 1:
                        squares(l, p, t - 1)
                    if t + 2 < T or following:
                        for h in range(2):
                            exp(l, e0 + (t + 2), (t + 2) % T, h)
                    if 1 <= t < T - 1:
                        squares(l, p, t - 1)
                    if t == 3:
                        mixT_high(l, p, 0, False)
                    if following and t == 1:
                        split_high(0, q_hi, following[0])
                        split_high(0, k_hi, following[1])
                    if following and t == 3:
                        split_high(1, q_hi, following[0])
                squares(l, p, T - 1)
                normed(l, p, T - 2)
                normed(l, p, T - 1)
                mixT_high(l, p, 1, False)

            early_squares(0, 0)
            with act.Fori(0, L) as l:
                high_at(l, 0)
                norm(l, 0, 1)
                n = 0
                for g, (_, _, k, _) in enumerate(PROJ):
                    for c in range(KT // k):
                        if g == G_KV and c == 0:
                            high_at(l, 2)
                            n += 1
                            continue
                        if g and c == 2:
                            for t in range(T):
                                copy_qkT(l, g - 1, t)
                        if g == G_DV and c == 1:
                            act.wait_ge(qkT_done.sem, qkT_done.at(l, 2 * T - 1))
                            for part in range(2):
                                split_high(part, q_hi, 0)
                                split_high(part, k_hi, 8)
                        if c == KT // k - 1:
                            read_projection(l, g)
                        if n + 1 < CHUNKS_IN:
                            high_at(l, n + 2)
                        n += 1
                for t in range(2):
                    for h in range(2):
                        exp(l, t, t, h)
                high_at(l, n + 1)
                with act.Fori(0, 2) as kv:
                    with act.Fori(0, 2) as r:
                        gqa_pair(l, kv * 2 + r, (kv * 2 + r + 1, kv + r + 8))
                with act.Fori(4, 7) as p:
                    diff_pair(l, p, (p + 1, p + 7))
                diff_pair(l, 7, None)
                for _ in range(CHUNKS_OUT - 1):
                    high_at(l, n + 2)
                    n += 1
                early_squares(l, 1)
                norm(l, 1, n + 2)
                f0 = 0
                for q, F in enumerate(FF_GROUPS):
                    nb = FFN_BASE[q]
                    with act.Fori(0, F // 2) as i:
                        for j in range(2):
                            e = i * 2 + (f0 + j)
                            act.wait_ge(gate_done.sem, gate_done.at(l, e))
                            act.wait_ge(actT_lo_done.sem, actT_lo_done.at(l, e - 2))
                            act.activation(silu[:, j, :, :], bank[:, 4 * j:4 * j + 2, 0:HALF_TOK],
                                           ACT.Silu).then_inc(silu_done.sem, 1)
                            m = nb + 2 * j + 2
                            high(l, m, i * (4 // RAW) + m // RAW, gate_done, e)
                            act.wait_ge(act_ready.sem, act_ready.at(l, e))
                            act.activation(one(actT_hi[:, at(i * 2 + j), :]),
                                           silu[:, j, :, :].rearrange("p a b -> p (a b)"),
                                           ACT.Copy).then_inc(actT_hi_done.sem, 1)
                            high(l, m + 1, i * (4 // RAW) + (m + 1) // RAW, up_done, e)
                    for m in range(nb + 2 * F, nb + 3 * F):
                        if m + 2 < CHUNKS:
                            high_at(l, m + 2)
                    f0 += F
                early_squares(l + 1, 0)
            for t in range(3, T):
                row_squares(L, 0, t)

        @block.vector
        def _(dve):
            def low(l, n0, n):
                dve.wait_ge(w_hi_done.sem, w_hi_done.at(l, n))
                dve.tensor_tensor(w_lo[n0 % SPLIT][:, :], w_raw[n0 % RAW][:, :], w_hi[n0 % SPLIT][:, :].bitcast(F32),
                                  ALU.subtract).then_inc(w_lo_done.sem, 1)

            def normed_row(l, m, t, free, free_value):
                dve.wait_ge(rstd_done.sem, rstd_done.at(l, m * T + t))
                if free is not None:
                    dve.wait_ge(free.sem, free_value)
                dve.scalar_tensor_tensor(h_row[:, t % 3, :], x[:, t, :], rstd[:, t:t + 1], gain[:, :], ALU.mult,
                                         ALU.mult).then_inc(h_ready.sem, 1)

            def late_row(l, m, t):
                normed_row(l, m, t, h_tr, h_tr.at(l, 2 * (m * T + t - 3) + 1))

            def transposed_low(l, m, t):
                for b in range(2):
                    e = 2 * (m * T + t) + b
                    dve.wait_ge(hT_hi_done.sem, hT_hi_done.at(l, e))
                    dst = (slice(None), slice(4 * b, 4 * b + 4), slice(t * P, (t + 1) * P))
                    dve.tensor_tensor(hT_lo[dst], bank[:, BANK_T + b, :].rearrange("p (k q) -> p k q", q=P),
                                      hT_hi[dst].bitcast(F32), ALU.subtract).then_inc(hT_lo_done.sem, 1)

            def add_and_norm(l, done, ed, c, next_l, m):
                dve.wait_ge(gain_loaded.sem, (next_l * 2 + (m + 1)) * 16)
                for t in range(T):
                    add_to_x(l, done, ed + t, t, c)
                    if 1 <= t <= 3:
                        normed_row(next_l, m, t - 1, None, None)
                    if m and t >= 3:
                        transposed_low(next_l, m, t - 3)

            def value_place(g, t):
                if g == G_KV:
                    return slice(0, P), bank[:, t, P:2 * P], v_rest_kv[t % 2]
                return slice(P, P + DIFF_V), bank[:, t, :], v_rest_dv[t % 2]

            def value_rest(l, g, t):
                e = t if g == G_KV else T + t
                cols, src, rest = value_place(g, t)
                dve.wait_ge(v0_done.sem, v0_done.at(l, e))
                if e >= 2:
                    dve.wait_ge(v2_done.sem, v2_done.at(l, e - 2))
                dve.tensor_tensor(rest, src, v[0][:, t, cols], ALU.subtract).then_inc(v_rest.sem, 1)

            def third_part(l, g, t):
                e = t if g == G_KV else T + t
                cols, _, rest = value_place(g, t)
                dve.wait_ge(v1_done.sem, v1_done.at(l, e))
                dve.tensor_tensor(v[2][:, t, cols], rest, v[1][:, t, cols], ALU.subtract).then_inc(v2_done.sem, 1)

            def head_sums(l, g, t):
                e = g * T + t
                heads = PROJ[g][3]
                dve.wait_ge(headsq_done.sem, headsq_done.at(l, e))
                dve.tensor_reduce(hss[:, t % 2, 0:heads], headsq[:, 0:heads * HD].rearrange("p (h d) -> p h d", d=HD),
                                  AX.X, ALU.add).then_inc(hss_done.sem, 1)

            def head_scale(l, g, t):
                e = g * T + t
                heads = PROJ[g][3]
                dve.wait_ge(hrstd_done.sem, hrstd_done.at(l, e))
                if e >= T:
                    dve.wait_ge(rot_tr.sem, rot_tr.at(l, e - T))
                dve.tensor_tensor(stage[:, t, 0:heads * HD].rearrange("p (h d) -> p h d", d=HD),
                                  bank[:, t, 0:heads * HD].rearrange("p (h d) -> p h d", d=HD),
                                  spread(hrstd[:, t % 2, 0:heads], 2, HD), ALU.mult).then_inc(scaled.sem, 1)

            def read_projection(l, g):
                if g == G_DV:
                    dve.wait_ge(rot_ready.sem, rot_ready.at(l, 4 * T - 1))
                for t in range(T + 1):
                    if t < T and g in (G_KV, G_Q):
                        head_sums(l, g, t)
                    if t < T and g in (G_KV, G_DV):
                        value_rest(l, g, t)
                    if t and g in (G_KV, G_Q):
                        head_scale(l, g, t - 1)
                    if t and g in (G_KV, G_DV):
                        third_part(l, g, t - 1)

            def rotate(l, g, t):
                e = g * T + t
                pos = seq_of(t)[2]
                heads = PROJ[g][3]
                W = heads * HD
                src = stage[:, t, 0:W]
                if g < 2:
                    i = 2 if g == G_KV else 0
                    dve.wait_ge(scaled.sem, scaled.at(l, e))
                    cos, sin = rope_g[:, i, pos, :], rope_g[:, i + 1, pos, :]
                    groups, half = 2, HD // 4
                else:
                    dve.wait_ge(copied.sem, copied.at(l, e - 2 * T))
                    cos, sin = rope[:, 0, pos, :], rope[:, 1, pos, :]
                    groups, half = 1, HD // 2
                if e:
                    dve.wait_ge(rot_ready.sem, rot_ready.at(l, e - 1))
                for a in range(2):
                    dve.tensor_tensor(
                        rope_t[:, 0:W].rearrange("p (h r a d) -> p h r a d", r=groups, a=2, d=half)[:, :, :, a, :],
                        src.rearrange("p (h r a d) -> p h r a d", r=groups, a=2, d=half)[:, :, :, 1 - a, :],
                        spread(sin.rearrange("p (r a d) -> p r a d", r=groups, a=2)[:, :, a, :], 1, heads), ALU.mult)
                dve.tensor_tensor(xn[:, 0:W].rearrange("p (h d) -> p h d", d=HD),
                                  src.rearrange("p (h d) -> p h d", d=HD), spread(cos, 1, heads),
                                  ALU.mult).then_inc(rope_t_done.sem, 1)
                dve.wait_ge(rope_t_done.sem, rope_t_done.at(l, e))
                if g == G_KV:
                    dve.tensor_tensor(stage[:, t, 0:2 * W].rearrange("p (h r d) -> p h r d", r=2, d=HD),
                                      spread(xn[:, 0:W].rearrange("p (h d) -> p h d", d=HD), 2, 2),
                                      spread(rope_t[:, 0:W].rearrange("p (h d) -> p h d", d=HD), 2, 2),
                                      ALU.add).then_inc(rot_ready.sem, 1)
                else:
                    dve.tensor_tensor(stage[:, t, :], xn[:, :], rope_t[:, :], ALU.add).then_inc(rot_ready.sem, 1)

            def row_max(l, e, t, h):
                S = seq_of(t)[1]
                b = t % 2
                dve.wait_ge(scores_done.sem, scores_done.at(l, e * 2 + h))
                dve.tensor_reduce(neg_max[:, b, h:h + 1], bank[:, 2 * b + h, 0:S], AX.X, ALU.max,
                                  negate=True).then_inc(max_done.sem, 1)

            def inverse_sums(l, e, t):
                dve.wait_ge(exp_done.sem, exp_done.at(l, e * 2 + 1))
                dve.reciprocal(inv_sum[:, t, :], row_sum[:, t, :]).then_inc(inv_done.sem, 1)

            def map_ratio(l, p, t):
                dve.wait_ge(inv_done.sem, inv_done.at(l, p * T + t))
                dve.scalar_tensor_tensor(ratio[:, t:t + 1], row_sum[:, t, 0:1], neg_lam[:, :], inv_sum[:, t, 1:2],
                                         ALU.mult, ALU.mult).then_inc(ratio_done.sem, 1)

            def combine(l, p, t):
                S = seq_of(t)[1]
                b = t % 2
                e = (p - 4) * T + t
                dve.wait_ge(ratio_done.sem, ratio_done.at(l, e))
                dve.scalar_tensor_tensor(prob[:, b, 0, 0:S], prob[:, b, 1, 0:S], ratio[:, t:t + 1],
                                         prob[:, b, 0, 0:S], ALU.mult, ALU.add).then_inc(p_comb.sem, 1)

            def probT_low(l, e, t, h, b, scale):
                nk = seq_of(t)[1] // P
                dve.wait_ge(pT_hi[h].sem, pT_hi[h].at(l, e))
                dve.scalar_tensor_tensor(probT[:, b, 1, 0:nk, :],
                                         bank[:, BANK_PT + b, 0:nk * P].rearrange("p (k q) -> p k q", q=P), scale,
                                         probT[:, b, 0, 0:nk, :], ALU.mult, ALU.subtract).then_inc(pT_lo[h].sem, 1)

            def mixT_low(l, p, part, gqa):
                t0, n = (0, 2) if part == 0 else (2, 4)
                dve.wait_ge(mixT_hi_done.sem, mixT_hi_done.at(l, p * 2 + part))
                dst, hi = one(hT_lo[:, at(p), t0 * P:(t0 + n) * P]), one(hT_hi[:, at(p), t0 * P:(t0 + n) * P]).bitcast(F32)
                if gqa:
                    i = dve.tensor_tensor(dst, bank[:, BANK_M, 0:n * P], hi, ALU.subtract)
                else:
                    i = dve.scalar_tensor_tensor(dst, bank[:, BANK_M, 0:n * P], sub_gain[:, :], hi, ALU.mult, ALU.subtract)
                i.then_inc(mixT_lo_done.sem, 1)

            def take_product(l, e, t):
                dve.wait_ge(o_done.sem, o_done.at(l, e))
                dve.scalar_tensor_tensor(mix[:, t, :].rearrange("p (h d) -> p h d", d=HD),
                                         bank[:, BANK_O + t % 2, 0:P].rearrange("p (h d) -> p h d", d=HD),
                                         1 / P_SCALE, spread(inv_sum[:, t, :], 2, HD), ALU.mult,
                                         ALU.mult).then_inc(mix_gqa.sem, 1)

            def next_maxima(l, e):
                for h in range(2):
                    row_max(l, e, 2, h)

            def gqa_pair(l, p):
                e0 = p * T
                for t in range(T):
                    if t >= 3:
                        row_max(l, e0 + (t + 1), (t + 1) % T, 1)
                    probT_low(l, e0 + t, t, 0, 0, P_SCALE)
                    inverse_sums(l, e0 + t, t)
                    if t >= 2 and t < T - 1:
                        row_max(l, e0 + (t + 2), (t + 2) % T, 0)
                    if t:
                        take_product(l, e0 + (t - 1), t - 1)
                    probT_low(l, e0 + t, t, 1, 1, P_SCALE)
                    if t == 0:
                        for h in range(2):
                            row_max(l, e0 + 3, 3, h)
                    if t == 2:
                        mixT_low(l, p, 0, True)
                for h in range(2):
                    row_max(l, e0 + (T + 1), 1, h)
                take_product(l, e0 + (T - 1), T - 1)
                next_maxima(l, e0 + (T + 2))
                mixT_low(l, p, 1, True)

            def second_map_in(l, p, t):
                inverse_sums(l, p * T + t, t)
                map_ratio(l, p, t)
                combine(l, p, t)

            def diff_pair(l, p, following):
                e0 = p * T
                for t in range(T):
                    ahead = t and (t + 2 < T or (following and t < T - 1))
                    combining = t and t + 1 < T
                    if combining:
                        inverse_sums(l, e0 + (t + 1), t + 1)
                    if ahead:
                        row_max(l, e0 + (t + 2), (t + 2) % T, 0)
                    if combining:
                        map_ratio(l, p, t + 1)
                    if ahead:
                        row_max(l, e0 + (t + 2), (t + 2) % T, 1)
                    if combining:
                        combine(l, p, t + 1)
                    probT_low(l, e0 + t, t, 0, t % 2, map_scale[:, :])
                    if t == 3:
                        mixT_low(l, p, 0, False)
                if following:
                    inverse_sums(l, e0 + T, 0)
                    row_max(l, e0 + (T + 1), 1, 0)
                    map_ratio(l, p + 1, 0)
                    row_max(l, e0 + (T + 1), 1, 1)
                    combine(l, p + 1, 0)
                    next_maxima(l, e0 + (T + 2))
                    second_map_in(l, p + 1, 1)
                mixT_low(l, p, 1, False)

            def layer_constants(l):
                dve.wait_ge(const_loaded.sem, 16 * 4)
                dve.tensor_copy(neg_lam[:, :], lam_dif[:, at(l)])
                dve.tensor_scalar(map_scale[:, :], lam_s[:, 1, at(l)], MAP_SCALE, None, ALU.mult)
                dve.tensor_scalar(eps_root[:, :], lam_s[:, 1, at(l)], MAP_SCALE * (2 * SUB_EPS) ** 0.5, None, ALU.mult)
                dve.tensor_tensor(sub_gain[:, :], sub_all[:, at(l)], laminit[:, 1, at(l)], ALU.mult)
                for i in range(2):
                    g = one(qk_gain[:, i, at(l), :])
                    dve.tensor_tensor(rope_g[:, 2 * i, :, :], rope[:, 2, :, :], spread(g, 1, 4), ALU.mult)
                    for a in range(2):
                        def part(ap, which):
                            return ap.rearrange("p t (r a d) -> p t r a d", r=2, a=2)[:, :, :, which, :]
                        gs = g.rearrange("p (r a d) -> p r a d", r=2, a=2)[:, :, 1 - a, :]
                        last = dve.tensor_tensor(part(rope_g[:, 2 * i + 1, :, :], a), part(rope[:, 3, :, :], a),
                                                 spread(gs, 1, 4), ALU.mult)
                last.then_inc(layer_consts.sem, 1)
                dve.wait_ge(layer_consts.sem, layer_consts.at(l, 0))

            def add_to_x(l, done, ed, t, c):
                dve.wait_ge(done.sem, done.at(l, ed))
                xs = x[:, t, c * COLS:(c + 1) * COLS]
                dve.tensor_tensor(xs, xs, bank[:, t, :], ALU.add).then_inc(x_added.sem, 1)

            dve.sem_inc(w_lo_done.sem, RAW)
            dve.sem_inc(w_used.sem, 1)
            dve.sem_inc(down_done.sem, 1)
            dve.sem_inc(mix_gqa.sem, 2)
            dve.sem_inc(mix_diff.sem, 2)
            dve.sem_inc(mixT_lo_done.sem, 1)
            dve.sem_inc(act_ready.sem, 2)
            dve.sem_inc(actT_lo_done.sem, 2)
            dve.sem_inc(x_added.sem, T)
            dve.wait_ge(lam_loaded.sem, 16)
            dve.wait_ge(laminit_loaded.sem, 16)
            pairs = lam_in[:, :, :, :].rearrange("p (s a) l d -> p s a (l d)", a=2)
            dve.tensor_tensor(lam_prod[:, :, :, :].rearrange("p s l d -> p s (l d)"), pairs[:, :, 0, :], pairs[:, :, 1, :],
                              ALU.mult).then_inc(setup.sem, 1)
            dve.wait_ge(setup.sem, 1)
            dve.tensor_reduce(lam_sum[:, :, :], lam_prod[:, :, :, :], AX.X, ALU.add).then_inc(setup.sem, 1)
            dve.wait_ge(lam_exp_done.sem, 1)
            dve.tensor_tensor(lam_dif[:, :], lam_exp[:, 1, :], lam_exp[:, 0, :], ALU.subtract).then_inc(setup.sem, 1)
            dve.wait_ge(setup.sem, 3)
            dve.tensor_tensor(lam_dif[:, :], lam_dif[:, :], laminit[:, 0, :], ALU.subtract).then_inc(setup.sem, 1)
            dve.wait_ge(setup.sem, 4)
            dve.tensor_scalar(lam_s[:, 0, :], lam_dif[:, :], -1.0, 1.0, ALU.mult, ALU.max).then_inc(setup.sem, 1)
            dve.wait_ge(setup.sem, 5)
            dve.tensor_tensor(lam_s[:, 0, :], lam_s[:, 0, :], lam_dif[:, :], ALU.max).then_inc(setup.sem, 1)
            dve.wait_ge(setup.sem, 6)
            dve.reciprocal(lam_s[:, 1, :], lam_s[:, 0, :]).then_inc(setup.sem, 1)
            dve.wait_ge(setup.sem, 7)

            dve.wait_ge(gain_loaded.sem, 16)
            for t in range(3):
                normed_row(0, 0, t, None, None)
            with dve.Fori(0, L) as l:
                low(l, 0, 0)
                transposed_low(l, 0, 0)
                late_row(l, 0, 3)
                transposed_low(l, 0, 1)
                late_row(l, 0, 4)
                low(l, 1, 1)
                transposed_low(l, 0, 2)
                late_row(l, 0, 5)
                for t in range(3, T):
                    transposed_low(l, 0, t)
                n = 0
                for g, (_, _, k, _) in enumerate(PROJ):
                    for c in range(KT // k):
                        if g == G_KV and c == 0:
                            low(l, 2, 2)
                            n += 1
                            continue
                        if g and c < 3:
                            rotate(l, g - 1, 2 * c)
                            rotate(l, g - 1, 2 * c + 1)
                        if c == KT // k - 1:
                            read_projection(l, g)
                        if n + 1 < CHUNKS_IN:
                            low(l, n + 2, n + 2)
                        if g == G_KV:
                            layer_constants(l)
                        n += 1
                for t in range(3):
                    for h in range(2):
                        row_max(l, t, t, h)
                low(l, n + 1, n + 1)
                with dve.Fori(0, 4) as p:
                    gqa_pair(l, p)
                for t in range(2):
                    second_map_in(l, 4, t)
                with dve.Fori(4, 7) as p:
                    diff_pair(l, p, True)
                diff_pair(l, 7, False)
                for c in range(2):
                    for kk in range(0, KT, 2):
                        last = kk == KT - 2
                        if last and c == 0:
                            for t in range(T):
                                add_to_x(l, out_done, t, t, 0)
                        if last and c:
                            add_and_norm(l, out_done, T, 1, l, 1)
                        else:
                            low(l, n + 2, n + 2)
                            n += 1
                late_row(l, 1, 3)
                late_row(l, 1, 4)
                low(l, n + 2, n + 2)
                transposed_low(l, 1, 3)
                late_row(l, 1, 5)
                transposed_low(l, 1, 4)
                transposed_low(l, 1, 5)
                f0 = 0
                for q, F in enumerate(FF_GROUPS):
                    nb = FFN_BASE[q]
                    with dve.Fori(0, F // 2) as i:
                        for j in range(2):
                            e = i * 2 + (f0 + j)
                            m = nb + 2 * j + 2
                            low(l, m, m + i * 4)
                            dve.wait_ge(up_done.sem, up_done.at(l, e))
                            dve.wait_ge(silu_done.sem, silu_done.at(l, e))
                            s = silu[:, j, :, :]
                            dve.tensor_tensor(s, s, bank[:, 4 * j + 2:4 * j + 4, 0:HALF_TOK],
                                              ALU.mult).then_inc(act_ready.sem, 1)
                            dve.wait_ge(actT_hi_done.sem, actT_hi_done.at(l, e))
                            dst = at(i * 2 + j)
                            dve.tensor_tensor(one(actT_lo[:, dst, :]), silu[:, j, :, :].rearrange("p a b -> p (a b)"),
                                              one(actT_hi[:, dst, :]).bitcast(F32),
                                              ALU.subtract).then_inc(actT_lo_done.sem, 1)
                            low(l, m + 1, m + 1 + i * 4)
                    for c in range(2):
                        for kk in range(0, F, 2):
                            m = nb + 2 * F + c * F // 2 + kk // 2
                            if kk == F - 2 and q == 2 and c:
                                add_and_norm(l, down_done, 5 * T, 1, l + 1, 0)
                            elif kk == F - 2:
                                for t in range(T):
                                    add_to_x(l, down_done, (2 * q + c) * T + t, t, c)
                            if m + 2 < CHUNKS:
                                low(l, m + 2, m + 2)
                    f0 += F
            for t in range(3, T):
                normed_row(L, 0, t, y_stored[t % 3], 16)

        @block.tensor
        def _(pe):
            def mm3(out, a_hi, a_lo, b_hi, b_lo, first, last):
                pe.matmul(out, a_hi, b_hi, start=first, stop=False)
                pe.matmul(out, a_hi, b_lo, start=False, stop=False)
                return pe.matmul(out, a_lo, b_hi, start=False, stop=last)

            def chunk(n0, k):
                s = n0 % SPLIT
                return (w_hi[s][:, :].rearrange("p (k c) -> p k c", k=k),
                        w_lo[s][:, :].rearrange("p (k c) -> p k c", k=k))

            def transpose_rows(l, m, t):
                e = m * T + t
                pe.wait_ge(h_ready.sem, h_ready.at(l, e))
                for b in range(2):
                    if e:
                        pe.wait_ge(hT_lo_done.sem, hT_lo_done.at(l, 2 * e + b - 2))
                    for k in range(4):
                        last = pe.transpose(bank[:, BANK_T + b, k * P:(k + 1) * P],
                                            h_row[:, t % 3, (4 * b + k) * P:(4 * b + k + 1) * P], ident[:, :])
                    last.then_inc(h_tr.sem, 1)

            def rows_product(l, t, n0, k, kt0, cols, srcT, first, last):
                hi, lo = chunk(n0, k)
                a_hi, a_lo = srcT
                for kk in range(k):
                    i = mm3(bank[:, t, 0:cols], a_hi[:, kt0 + kk, t * P:(t + 1) * P], a_lo[:, kt0 + kk, t * P:(t + 1) * P],
                            hi[:, kk, :], lo[:, kk, :], first and kk == 0, last and kk == k - 1)
                return i

            def scores(l, e, t, h, split=None, first=False):
                k0, S, _ = seq_of(t)
                b = t % 2
                if split is not None:
                    pe.wait_ge(qk_split.sem, qk_split.at(l, split * 2 + 1))
                if not first:
                    pe.wait_ge(exp_done.sem, exp_done.at(l, (e - 2) * 2 + h))
                rows = slice(h * HD, (h + 1) * HD)
                mm3(bank[:, 2 * b + h, 0:S], q_hi[rows, t * P:(t + 1) * P], q_lo[rows, t * P:(t + 1) * P],
                    k_hi[rows, k0:k0 + S], k_lo[rows, k0:k0 + S], True, True).then_inc(scores_done.sem, 1)

            def transpose_mix(l, p, part, gqa):
                t0, n = (0, 2) if part == 0 else (2, 4)
                if gqa:
                    pe.wait_ge(mix_gqa.sem, mix_gqa.at(l, p * T + (t0 + n - 1)))
                else:
                    pe.wait_ge(mix_diff.sem, mix_diff.at(l, (p - 4) * T + (t0 + n - 1)))
                for t in range(n):
                    last = pe.transpose(bank[:, BANK_M, t * P:(t + 1) * P], mix[:, t0 + t, :], ident[:, :])
                last.then_inc(mix_tr.sem, 1)

            def transpose_prob(t, h, b):
                for k in range(seq_of(t)[1] // P):
                    last = pe.transpose(bank[:, BANK_PT + b, k * P:(k + 1) * P],
                                        prob[:, t % 2, h, k * P:(k + 1) * P], ident[:, :])
                last.then_inc(pT_tr[h].sem, 1)

            def product(t, out, b, vcol, width):
                k0, S, _ = seq_of(t)
                terms = [(k, a, i) for k in range(S // P) for a, i in ((0, 0), (0, 1), (0, 2), (1, 0), (1, 1))]
                for k, a, i in terms:
                    last = pe.matmul(out, probT[:, b, a, k, :], v[i][:, k0 // P + k, at(vcol, width)],
                                     start=(k, a, i) == terms[0], stop=(k, a, i) == terms[-1])
                return last

            def gqa_transpose(l, e, t, h):
                pe.wait_ge(exp_done.sem, exp_done.at(l, e * 2 + h))
                transpose_prob(t, h, h)

            def bank_free_of_mix(l, p, t):
                if t in (1, 3):
                    pe.wait_ge(mixT_lo_done.sem, mixT_lo_done.at(l, p * 2 + (t // 2 - 1)))

            def gqa_product(l, p, t, h, vcol):
                e = p * T + t
                if h == 0:
                    pe.wait_ge(mix_gqa.sem, mix_gqa.at(l, e - 2))
                    bank_free_of_mix(l, p, t)
                pe.wait_ge(pT_lo[h].sem, pT_lo[h].at(l, e))
                last = product(t, bank[:, BANK_O + t % 2, h * HD:(h + 1) * HD], h, vcol, HD)
                if h:
                    last.then_inc(o_done.sem, 1)

            def gqa_pair(l, p, vcol):
                e0 = p * T
                pe.wait_ge(v_rest.sem, v_rest.at(l, 2 * T - 1))
                pe.wait_ge(qkT_done.sem, qkT_done.at(l, 4 * T - 1))
                for t in range(T - 1):
                    e = e0 + t
                    for h in range(2):
                        gqa_transpose(l, e, t, h)
                        if t == 0 and h:
                            scores(l, e + 3, 3, 0)
                            scores(l, e + 3, 3, 1)
                        if t >= 2:
                            scores(l, e + 2, (t + 2) % T, h, p * 2 + 2 if t == 4 and h == 0 else None)
                        if h:
                            gqa_product(l, p, t, 0, vcol)
                        elif t:
                            gqa_product(l, p, t - 1, 1, vcol)
                    if t == 2:
                        transpose_mix(l, p, 0, True)
                e, t = e0 + (T - 1), T - 1
                gqa_transpose(l, e, t, 0)
                gqa_product(l, p, T - 2, 1, vcol)
                gqa_transpose(l, e, t, 1)
                scores(l, e0 + (T + 1), 1, 0)
                gqa_product(l, p, t, 0, vcol)
                scores(l, e0 + (T + 1), 1, 1)
                gqa_product(l, p, t, 1, vcol)
                scores(l, e0 + (T + 2), 2, 0, p * 2 + 3)
                scores(l, e0 + (T + 2), 2, 1)
                transpose_mix(l, p, 1, True)

            def diff_transpose(l, p, t):
                pe.wait_ge(p_comb.sem, p_comb.at(l, (p - 4) * T + t))
                transpose_prob(t, 0, t % 2)

            def diff_product(l, p, t, vcol):
                e = (p - 4) * T + t
                pe.wait_ge(mix_diff.sem, mix_diff.at(l, e - 2))
                bank_free_of_mix(l, p, t)
                pe.wait_ge(pT_lo[0].sem, pT_lo[0].at(l, p * T + t))
                product(t, bank[:, BANK_O + t % 2, 0:P], t % 2, vcol, P).then_inc(o_done.sem, 1)

            def diff_pair(l, p, following, vcol):
                e0 = p * T
                pe.wait_ge(v2_done.sem, v2_done.at(l, 2 * T - 1))
                for t in range(T - 1):
                    if t and (t + 2 < T or following):
                        for h in range(2):
                            scores(l, e0 + (t + 2), (t + 2) % T, h, p * 2 + 2 if t == 4 and h == 0 else None)
                    diff_transpose(l, p, t)
                    if t:
                        diff_product(l, p, t - 1, vcol)
                    if t == 3:
                        transpose_mix(l, p, 0, False)
                diff_transpose(l, p, T - 1)
                if following:
                    scores(l, e0 + (T + 1), 1, 0)
                    scores(l, e0 + (T + 1), 1, 1)
                diff_product(l, p, T - 2, vcol)
                diff_product(l, p, T - 1, vcol)
                if following:
                    scores(l, e0 + (T + 2), 2, 0, p * 2 + 3)
                    scores(l, e0 + (T + 2), 2, 1)
                transpose_mix(l, p, 1, False)

            hT = (hT_hi, hT_lo)
            actT = (actT_hi, actT_lo)
            pe.wait_ge(ident_loaded.sem, 16)
            with pe.Fori(0, L) as l:
                def proj_product(g, t, c, n):
                    _, cols, k, _ = PROJ[g]
                    last = c == KT // k - 1
                    i = rows_product(l, t, n, k, c * k, cols, hT, c == 0, last)
                    if last:
                        i.then_inc(proj_done.sem, 1)
                    elif t == T - 1:
                        i.then_inc(w_used.sem, 1)

                transpose_rows(l, 0, 0)
                for t in range(T + 2):
                    if t < T:
                        if t + 1 < T:
                            transpose_rows(l, 0, t + 1)
                        if t == 0:
                            pe.wait_ge(w_lo_done.sem, w_lo_done.at(l, 0))
                        pe.wait_ge(hT_lo_done.sem, hT_lo_done.at(l, 2 * t + 1))
                        proj_product(G_KV, t, 0, 0)
                    if t == 2:
                        pe.wait_ge(w_lo_done.sem, w_lo_done.at(l, 1))
                    if t >= 2:
                        proj_product(G_KV, t - 2, 1, 1)
                n = 2
                for g in range(1, len(PROJ)):
                    for c in range(4):
                        pe.wait_ge(w_lo_done.sem, w_lo_done.at(l, n))
                        for t in range(T):
                            if c == 0:
                                if g - 1 < 2:
                                    pe.wait_ge(scaled.sem, scaled.at(l, (g - 1) * T + t))
                                else:
                                    pe.wait_ge(copied.sem, copied.at(l, (g - 3) * T + t))
                            proj_product(g, t, c, n)
                            if c == 2:
                                e = (g - 1) * T + t
                                pe.wait_ge(rot_ready.sem, rot_ready.at(l, e))
                                if e >= 2:
                                    pe.wait_ge(qkT_done.sem, qkT_done.at(l, e - 2))
                                for b in range(N_BLOCKS[g - 1]):
                                    last = pe.transpose(bank[:, BANK_T + t % 2, b * P:(b + 1) * P],
                                                        stage[:, t, b * P:(b + 1) * P], ident[:, :])
                                last.then_inc(rot_tr.sem, 1)
                        n += 1
                for t in range(3):
                    if t < 2:
                        pe.wait_ge(v_rest.sem, v_rest.at(l, T + 2 * t + 1))
                    for h in range(2):
                        scores(l, t, t, h, {(0, 0): 0, (2, 0): 1}.get((t, h)), first=t < 2)
                with pe.Fori(0, 2) as kv:
                    with pe.Fori(0, 2) as r:
                        gqa_pair(l, kv * 2 + r, kv * HD)
                with pe.Fori(4, 7) as p:
                    diff_pair(l, p, True, p * P - 3 * P)
                diff_pair(l, 7, False, 4 * P)
                pe.wait_ge(mixT_lo_done.sem, mixT_lo_done.at(l, 2 * PAIRS - 1))
                for c in range(2):
                    for kk in range(0, KT, 2):
                        pe.wait_ge(w_lo_done.sem, w_lo_done.at(l, n))
                        for t in range(T):
                            if c and kk == 0:
                                pe.wait_ge(x_added.sem, x_added.at(l, t))
                            i = rows_product(l, t, n, 2, kk, COLS, hT, kk == 0, kk == KT - 2)
                            if kk == KT - 2:
                                i.then_inc(out_done.sem, 1)
                            elif t == T - 1:
                                i.then_inc(w_used.sem, 1)
                            if c and kk == KT - 2 and t >= 3:
                                transpose_rows(l, 1, t - 3)
                        n += 1
                def gate_up(m, done, u, j, i, halves, finish, between=None):
                    pe.wait_ge(w_lo_done.sem, w_lo_done.at(l, i * 4 + m))
                    a_hi, a_lo = chunk(m, KT)
                    for half in halves:
                        cols = slice(half * HALF_TOK, (half + 1) * HALF_TOK)
                        for k in range(KT):
                            last = mm3(bank[:, 4 * j + 2 * u + half, 0:HALF_TOK], a_hi[:, k, :], a_lo[:, k, :],
                                       hT_hi[:, k, cols], hT_lo[:, k, cols], k == 0, k == KT - 1)
                            if between and k in between:
                                transpose_rows(l, 1, between[k])
                    if finish:
                        last.then_inc(done.sem, 1)

                def ff_tile(q, i, j, f0):
                    e = i * 2 + (f0 + j)
                    if q:
                        pe.wait_ge(x_added.sem, x_added.at(l, (2 * q + 2) * T - 1))
                    pe.wait_ge(act_ready.sem, act_ready.at(l, e - 2))
                    for u, done in enumerate((gate_done, up_done)):
                        gate_up(FFN_BASE[q] + 2 * j + u, done, u, j, i, (0, 1), True)

                pe.wait_ge(hT_lo_done.sem, hT_lo_done.at(l, 2 * (T + T // 2) - 1))
                pe.wait_ge(act_ready.sem, act_ready.at(l, -2))
                gate_up(FFN_BASE[0], gate_done, 0, 0, 0, (0,), False, {3: 3, 7: 4})
                gate_up(FFN_BASE[0] + 1, up_done, 1, 0, 0, (0,), False, {3: 5})
                pe.wait_ge(hT_lo_done.sem, hT_lo_done.at(l, 4 * T - 1))
                gate_up(FFN_BASE[0], gate_done, 0, 0, 0, (1,), True)
                gate_up(FFN_BASE[0] + 1, up_done, 1, 0, 0, (1,), True)
                ff_tile(0, 0, 1, 0)
                f0 = 0
                for q, F in enumerate(FF_GROUPS):
                    nb = FFN_BASE[q]
                    with pe.Fori(0 if q else 1, F // 2) as i:
                        for j in range(2):
                            ff_tile(q, i, j, f0)
                    for c in range(2):
                        for kk in range(0, F, 2):
                            m = nb + 2 * F + c * F // 2 + kk // 2
                            pe.wait_ge(w_lo_done.sem, w_lo_done.at(l, m))
                            if c == 0:
                                pe.wait_ge(actT_lo_done.sem, actT_lo_done.at(l, f0 + kk + 1))
                            for t in range(T):
                                if kk == 0 and c == 0 and t in (0, 4):
                                    pe.wait_ge(act_ready.sem, act_ready.at(l, f0 + F - 2 + t // 4))
                                if kk == 0 and c:
                                    pe.wait_ge(x_added.sem, x_added.at(l, (2 * q + 2) * T + t))
                                last = rows_product(l, t, m, 2, kk, COLS, actT, kk == 0, kk == F - 2)
                                if kk == F - 2:
                                    last.then_inc(down_done.sem, 1)
                                elif t == T - 1:
                                    last.then_inc(w_used.sem, 1)
                    f0 += F


_INS = ["x_prompt", "x_sample", "w_in", "w_out", "gqa_q_norm", "gqa_k_norm", "lam_vectors", "sub_gains", "gains", "w_gate_up", "w_down"]
_OUTS = [(1, T_PROMPT * P, D), (1, T_SAMPLE * P, D)]


def _shape_constants():
    import numpy as np
    import math
    f = np.float32

    def angles(pos, dim):
        inv = f(10000.0) ** (-np.arange(0, dim, 2, dtype=f) / f(dim))
        ang = pos.astype(f)[:, None] * inv[None, :].astype(f)
        return np.cos(ang).astype(f), np.sin(ang).astype(f)

    t = np.arange(T_SAMPLE * P)
    tc, ts = angles(t, HD)
    rc, rs = angles(t // 64, HD // 2)
    cc, cs = angles(t % 64, HD // 2)
    tables = np.stack([np.concatenate([tc, tc], 1), np.concatenate([-ts, ts], 1),
                       np.concatenate([rc, rc, cc, cc], 1), np.concatenate([-rs, rs, -cs, cs], 1)])
    rope = np.ascontiguousarray(tables.reshape(4, T_SAMPLE, P, HD).transpose(2, 0, 1, 3)).astype(f)
    init = [0.8 - 0.6 * math.exp(-0.3 * l) for l in range(L)]
    laminit = np.broadcast_to(np.array([init, [(1.0 - i) * math.sqrt(2.0) for i in init]], f), (P, 2, L)).copy()
    return {"ident": np.eye(P, dtype=f), "rope": rope, "laminit": laminit}


def kernel(**inputs):
    import numpy as _np
    import concourse.bacc as _bacc
    from concourse import mybir as _mybir
    from concourse.bass_utils import run_bass_kernel_spmd as _run

    per_layer = _np.stack([_np.asarray(inputs["attn_norm"]), _np.asarray(inputs["ffn_norm"])], axis=1)
    inputs["gains"] = _np.concatenate([per_layer.reshape(2 * L, D), _np.asarray(inputs["final_norm"])[None]], axis=0)
    inputs["lam_vectors"] = _np.stack([_np.asarray(inputs[f"diff_lambda_{n}"]) for n in ("q1", "k1", "q2", "k2")])
    inputs["sub_gains"] = _np.asarray(inputs["diff_sub_norm"]).T
    nc = _bacc.Bacc("TRN2", target_bir_lowering=False, num_devices=1)
    arrays, args = {}, []
    for name, a in [(n, inputs[n]) for n in _INS] + list(_shape_constants().items()):
        a = _np.ascontiguousarray(a)
        arrays[f"in_{name}_dram"] = a
        args.append(nc.dram_tensor(f"in_{name}_dram", a.shape, _mybir.dt.from_np(a.dtype), kind="ExternalInput").ap())
    for i, shape in enumerate(_OUTS):
        args.append(nc.dram_tensor(f"out_{i}_dram", shape, _mybir.dt.float32, kind="ExternalOutput").ap())
    build(nc, *args)
    r = _run(nc, [arrays], core_ids=[0])
    return tuple(r.results[0][f"out_{i}_dram"] for i in range(len(_OUTS)))
```
